# Optimizing a Trainium2 kernel written in Bass

```python
import math
import jax, jax.numpy as jnp
from jax import lax
import numpy as np

D_MODEL = 2048
BATCH = 1
SEQ = 256
DEPTH = 1

MEM_LEN = 256

MIX_WIDTH = D_MODEL
POOL_WIDTH = D_MODEL // 4
POOL_WINDOWS = (2, 4, 8, 16)
POOL_GROUP = POOL_WIDTH // len(POOL_WINDOWS)
SWA_HEAD_DIM = 64
SWA_WIDTH = D_MODEL // 2
SWA_HEADS = SWA_WIDTH // SWA_HEAD_DIM
SWA_KV_HEADS = 4
SWA_KV_WIDTH = SWA_KV_HEADS * SWA_HEAD_DIM
WINDOW = 128
BLOCK = 128
ROPE_THETA = 500000.0
ROPE_DIM = SWA_HEAD_DIM // 4
MEM_HEADS = 4
MEM_WIDTH = D_MODEL // 4
MEM_HEAD_DIM = MEM_WIDTH // MEM_HEADS
IN_WIDTH = POOL_WIDTH + SWA_WIDTH + 2 * SWA_KV_WIDTH + MEM_WIDTH

PEER_HEADS = 8
N_KEYS = 128
N_EXPERTS = N_KEYS * N_KEYS
PEER_TOPK = 16
QUERY_DIM = 256
HALF_DIM = QUERY_DIM // 2
PEER_CHUNK = 128

ALPHA = (2.0 * DEPTH) ** 0.25
BETA = (8.0 * DEPTH) ** -0.25
LN_EPS = 1e-5
NEG = -1e30

kernel_name = "hymba_pool_swa_mem_peer_deepnorm"

def layer_norm(x, g, b):
    xf = x.astype(jnp.float32)
    mu = xf.mean(-1, keepdims=True)
    var = jnp.square(xf - mu).mean(-1, keepdims=True)
    y = (xf - mu) * lax.rsqrt(var + LN_EPS) * g.astype(jnp.float32) + b.astype(jnp.float32)
    return y.astype(x.dtype)

def partial_rope(t, positions):
    half = ROPE_DIM // 2
    inv_freq = ROPE_THETA ** (-jnp.arange(0, ROPE_DIM, 2, dtype=jnp.float32) / ROPE_DIM)
    ang = positions.astype(jnp.float32)[:, :, None] * inv_freq
    cos = jnp.cos(ang)[:, :, None, :]
    sin = jnp.sin(ang)[:, :, None, :]
    tf = t.astype(jnp.float32)
    t1, t2, rest = tf[..., :half], tf[..., half:ROPE_DIM], tf[..., ROPE_DIM:]
    out = jnp.concatenate([t1 * cos - t2 * sin, t2 * cos + t1 * sin, rest], axis=-1)
    return out.astype(t.dtype)

def multiscale_pool(v, w_pool, pool_scale):
    B, S, C = v.shape
    vf = v.astype(jnp.float32)
    csum = jnp.cumsum(vf, axis=1)
    outs = []
    for g, w in enumerate(POOL_WINDOWS):
        sl = slice(g * POOL_GROUP, (g + 1) * POOL_GROUP)
        cg = csum[..., sl]
        shifted = jnp.pad(cg, ((0, 0), (w, 0), (0, 0)))[:, :S]
        count = jnp.minimum(jnp.arange(1, S + 1), w).astype(jnp.float32)[None, :, None]
        outs.append((cg - shifted) / count - vf[..., sl])
    pooled = jnp.stack(outs, axis=2).astype(v.dtype)
    y = jnp.einsum('bsgc,gcd->bsgd', pooled, w_pool).reshape(B, S, C)
    return y * pool_scale

def sliding_window_attention(q, k, v, sinks):
    B, S, H, Dh = q.shape
    KV = SWA_KV_HEADS
    G = H // KV
    nb = S // BLOCK
    qb = q.reshape(B, nb, BLOCK, KV, G, Dh)
    pad = jnp.zeros((B, BLOCK, KV, Dh), k.dtype)
    kp = jnp.concatenate([pad, k], axis=1).reshape(B, nb + 1, BLOCK, KV, Dh)
    vp = jnp.concatenate([pad, v], axis=1).reshape(B, nb + 1, BLOCK, KV, Dh)
    kb = jnp.concatenate([kp[:, :-1], kp[:, 1:]], axis=2)
    vb = jnp.concatenate([vp[:, :-1], vp[:, 1:]], axis=2)
    s = jnp.einsum('bnqkgd,bnskd->bnkgqs', qb, kb).astype(jnp.float32) * (Dh ** -0.5)
    blk = jnp.arange(nb)[:, None] * BLOCK
    q_pos = blk + jnp.arange(BLOCK)[None, :]
    k_pos = blk - BLOCK + jnp.arange(2 * BLOCK)[None, :]
    rel = q_pos[:, :, None] - k_pos[:, None, :]
    valid = (rel >= 0) & (rel < WINDOW) & (k_pos[:, None, :] >= 0)
    s = jnp.where(valid[None, :, None, None], s, NEG)
    sink = sinks.astype(jnp.float32).reshape(KV, G)[None, None, :, :, None, None]
    m = jnp.maximum(s.max(-1, keepdims=True), sink)
    p = jnp.exp(s - m)
    p = p / (p.sum(-1, keepdims=True) + jnp.exp(sink - m))
    o = jnp.einsum('bnkgqs,bnskd->bnqkgd', p.astype(v.dtype), vb)
    return o.reshape(B, S, H * Dh)

def memory_attention(qm, km, vm):
    B, S = qm.shape[:2]
    s = jnp.einsum('bshd,bmhd->bhsm', qm, km).astype(jnp.float32) * (MEM_HEAD_DIM ** -0.5)
    p = jax.nn.softmax(s, axis=-1).astype(vm.dtype)
    o = jnp.einsum('bhsm,bmhd->bshd', p, vm)
    return o.reshape(B, S, MEM_WIDTH)

def peer(x, w_peer_q, sub_keys_1, sub_keys_2, expert_u, expert_v):
    B, S, D = x.shape
    q = (x @ w_peer_q).reshape(B, S, PEER_HEADS, 2, HALF_DIM)
    s1 = jnp.einsum('bshc,kc->bshk', q[..., 0, :], sub_keys_1).astype(jnp.float32)
    s2 = jnp.einsum('bshc,kc->bshk', q[..., 1, :], sub_keys_2).astype(jnp.float32)
    v1, i1 = lax.top_k(s1, PEER_TOPK)
    v2, i2 = lax.top_k(s2, PEER_TOPK)
    cand_s = (v1[..., :, None] + v2[..., None, :]).reshape(B, S, PEER_HEADS, PEER_TOPK * PEER_TOPK)
    cand_i = (i1[..., :, None] * N_KEYS + i2[..., None, :]).reshape(B, S, PEER_HEADS, PEER_TOPK * PEER_TOPK)
    top_s, pos = lax.top_k(cand_s, PEER_TOPK)
    idx = jnp.take_along_axis(cand_i, pos, axis=-1)
    gate = jax.nn.softmax(top_s, axis=-1).astype(x.dtype)
    T = B * S
    nc = T // PEER_CHUNK
    E = PEER_HEADS * PEER_TOPK
    xc = x.reshape(nc, PEER_CHUNK, D)
    ic = idx.reshape(nc, PEER_CHUNK, E)
    gc = gate.reshape(nc, PEER_CHUNK, E)

    def block(args):
        xb, ib, gb = args
        u = expert_u[ib]
        h = jnp.einsum('cd,ced->ce', xb, u)
        a = gb * jax.nn.gelu(h, approximate=False)
        return jnp.einsum('ce,ced->cd', a, expert_v[ib])

    out = lax.map(block, (xc, ic, gc))
    return out.reshape(B, S, D)

def setup_inputs(seed: int = 0) -> dict:
    key = jax.random.key(seed)
    ks = jax.random.split(key, 20)
    f32 = jnp.float32
    L, D = DEPTH, D_MODEL
    nrm = lambda k, shape, scale: jax.random.normal(k, shape, f32) * scale
    return {
        "x": nrm(ks[0], (BATCH, SEQ, D), 1.0),
        "mem": nrm(ks[1], (BATCH, MEM_LEN, D), 1.0),
        "positions": jnp.broadcast_to(jnp.arange(SEQ, dtype=jnp.int32)[None, :], (BATCH, SEQ)),
        "w_in": nrm(ks[2], (L, D, IN_WIDTH), D ** -0.5),
        "w_mem_kv": nrm(ks[3], (L, D, 2 * MEM_WIDTH), D ** -0.5),
        "w_pool": nrm(ks[4], (L, len(POOL_WINDOWS), POOL_GROUP, POOL_GROUP), POOL_GROUP ** -0.5),
        "pool_scale": 1.0 + nrm(ks[5], (L, POOL_WIDTH), 0.02),
        "attn_sinks": nrm(ks[6], (L, SWA_HEADS), 0.5),
        "w_out": nrm(ks[7], (L, MIX_WIDTH, D), BETA * MIX_WIDTH ** -0.5),
        "ln1_g": 1.0 + nrm(ks[8], (L, D), 0.02),
        "ln1_b": nrm(ks[9], (L, D), 0.02),
        "w_peer_q": nrm(ks[10], (L, D, PEER_HEADS * QUERY_DIM), D ** -0.5),
        "sub_keys_1": nrm(ks[11], (L, N_KEYS, HALF_DIM), HALF_DIM ** -0.5),
        "sub_keys_2": nrm(ks[12], (L, N_KEYS, HALF_DIM), HALF_DIM ** -0.5),
        "expert_u": nrm(ks[13], (L, N_EXPERTS, D), D ** -0.5),
        "expert_v": nrm(ks[14], (L, N_EXPERTS, D), BETA),
        "ln2_g": 1.0 + nrm(ks[15], (L, D), 0.02),
        "ln2_b": nrm(ks[16], (L, D), 0.02),
    }

def reference(x, mem, positions, w_in, w_mem_kv, w_pool, pool_scale, attn_sinks, w_out,
              ln1_g, ln1_b, w_peer_q, sub_keys_1, sub_keys_2, expert_u, expert_v, ln2_g, ln2_b):
    B, S, D = x.shape
    offs = np.cumsum([POOL_WIDTH, SWA_WIDTH, SWA_KV_WIDTH, SWA_KV_WIDTH]).tolist()
    for l in range(DEPTH):
        h = x @ w_in[l]
        pool_v, q, k, v, qm = jnp.split(h, offs, axis=-1)
        pool_out = multiscale_pool(pool_v, w_pool[l], pool_scale[l])
        q = partial_rope(q.reshape(B, S, SWA_HEADS, SWA_HEAD_DIM), positions)
        k = partial_rope(k.reshape(B, S, SWA_KV_HEADS, SWA_HEAD_DIM), positions)
        v = v.reshape(B, S, SWA_KV_HEADS, SWA_HEAD_DIM)
        swa_out = sliding_window_attention(q, k, v, attn_sinks[l])
        kvm = mem @ w_mem_kv[l]
        km, vm = jnp.split(kvm, 2, axis=-1)
        Mn = mem.shape[1]
        mem_out = memory_attention(qm.reshape(B, S, MEM_HEADS, MEM_HEAD_DIM),
                                   km.reshape(B, Mn, MEM_HEADS, MEM_HEAD_DIM),
                                   vm.reshape(B, Mn, MEM_HEADS, MEM_HEAD_DIM))
        mix = jnp.concatenate([pool_out, swa_out, mem_out], axis=-1) @ w_out[l]
        x = layer_norm(ALPHA * x + mix, ln1_g[l], ln1_b[l])
        ff = peer(x, w_peer_q[l], sub_keys_1[l], sub_keys_2[l], expert_u[l], expert_v[l])
        x = layer_norm(ALPHA * x + ff, ln2_g[l], ln2_b[l])
    return x


_drawn_inputs = setup_inputs


def setup_inputs(seed=0):
    import zlib

    import numpy as np

    out = dict(_drawn_inputs(seed))
    spreads = {}
    factors = {'pool_scale': 3.211, 'attn_sinks': 7.125, 'ln2_g': 2.748, 'ln2_b': 2.902}
    for name, (base, spread) in spreads.items():
        noise = np.random.default_rng([zlib.crc32(name.encode()), seed]).standard_normal(out[name].shape)
        drawn = base * np.exp(spread * noise) if base else spread * noise
        out[name] = __import__('jax').numpy.asarray(drawn.astype(out[name].dtype))
    for name, factor in factors.items():
        out[name] = (out[name] * factor).astype(out[name].dtype)
    return out
```

```python
import concourse.bass as bass
from concourse import mybir
from contextlib import ExitStack

F32 = mybir.dt.float32
F32R = mybir.dt.float32r
I32 = mybir.dt.int32
U32 = mybir.dt.uint32
ALU = mybir.AluOpType
ACT = mybir.ActivationFunctionType
AX = mybir.AxisListType

P = 128
D = 2048
S = 256
T = S // P
KC = D // P
POOL_W, SWA_W, KV_W, MEM_W = 512, 1024, 256, 512
WINDOWS = (2, 4, 8, 16)
PAD = WINDOWS[-1]
HEADS, HD = 16, 64
MHEADS, MHD = 4, 128
ROPE = HD // 4
HALF = ROPE // 2
THETA = 500000.0
PHEADS, KEYS, TOPK = 8, 128, 16
PICKS = PHEADS * TOPK
ALPHA = 2.0 ** 0.25
EPS = 1e-5
NEG = -1e30
LOWEST = -3.0e38
PI = 3.14159265358979
ROUND = 12582912.0
TWO_PI = (6.28125, 0.0019350051879882812, 3.0199159819e-07)

COLS = 1024
PAIR = 2
UNITS = KC // PAIR
RAW = 2
SPLIT = 2
RING = 8
PRESET = RING + TOPK

GROUPS = (
    ("q", "RR"),
    ("kv", "R"),
    ("mem", "TR"),
    ("pool_qm", "TT"),
    ("out0", "RR"),
    ("out1", "RR"),
    ("peer0", "TT"),
    ("peer1", "TT"),
)
Q, KV, MEM, POOLQM, OUT0, OUT1, PEER0, PEER1 = range(len(GROUPS))


def hybrid_layer(nc, x, mem, positions, w_in, w_mem_kv, w_pool, pool_scale, attn_sinks, w_out, ln1_g, ln1_b,
                 w_peer_q, sub_keys_1, sub_keys_2, expert_u, expert_v, ln2_g, ln2_b, out):
    ctx = ExitStack()
    with ctx:
        def sb(name, shape, dt, where=ctx):
            return where.enter_context(nc.sbuf_tensor(name, shape, dt))

        def sem(name):
            return ctx.enter_context(nc.semaphore(name))

        resid = sb("resid", [P, T, D], F32)
        scores_sb = sb("scores_sb", [P, HEADS, S], F32)
        ident = sb("ident", [P, P], F32)
        keysT = sb("keysT", [P, 2, KEYS], F32)
        stats = sb("stats", [P, T, 4, 6], F32)
        moments = sb("moments", [P, T, 2], F32)
        rstd = sb("rstd", [P, T, 4], F32)
        iota16 = sb("iota16", [P, TOPK], F32)
        ps = ctx.enter_context(nc.psum_tensor("ps", [P, 8, 512], F32))

        mix = ExitStack()
        probs = sb("probs", [P, HEADS, S], F32, mix)
        xT_hi = sb("xT_hi", [P, KC, S], F32R, mix)
        xT_lo = sb("xT_lo", [P, KC, S], F32R, mix)
        yT_hi = sb("yT_hi", [P, KC, S], F32R, mix)
        yT_lo = sb("yT_lo", [P, KC, S], F32R, mix)
        raw = sb("raw", [P, RAW, PAIR, COLS], F32, mix)
        w_hi_sb = sb("w_hi_sb", [P, SPLIT, PAIR, COLS], F32R, mix)
        w_lo_sb = sb("w_lo_sb", [P, SPLIT, PAIR, COLS], F32R, mix)
        kv = sb("kv", [P, T, 2 * KV_W], F32, mix)
        qT = sb("qT", [P, HEADS // 2, S], F32, mix)
        kT = sb("kT", [P, 2, S], F32, mix)
        qmT = sb("qmT", [P, MHEADS, S], F32, mix)
        kmT = sb("kmT", [P, MHEADS, S], F32, mix)
        vm = sb("vm", [P, T, MEM_W], F32, mix)
        win_a = sb("win_a", [P, 4, PAD + S], F32, mix)
        pT = sb("pT", [P, 2, 512], F32, mix)
        w_pool_sb = sb("w_pool_sb", [P, 4, P], F32, mix)
        keys_rows = sb("keys_rows", [P, 2, KEYS], F32, mix)
        mask = sb("mask", [P, 2, P], F32, mix)
        scale_sb = sb("scale_sb", [P, 4], F32, mix)
        sinks = sb("sinks", [P, HEADS], F32, mix)
        pos_i = sb("pos_i", [P, T], I32, mix)
        pos_f = sb("pos_f", [P, T], F32, mix)
        ang = sb("ang", [P, 2, T, HALF], F32, mix)
        turns = sb("turns", [P, 2, T, HALF], F32, mix)
        cossin = sb("cossin", [P, 2, T, HALF], F32, mix)
        rt = sb("rt", [P, 4, HEADS * HALF], F32, mix)
        inv_count = sb("inv_count", [P, PAD], F32, mix)
        edge = sb("edge", [P, PAD], F32, mix)
        row_max = sb("row_max", [P, HEADS], F32, mix)
        neg_max = sb("neg_max", [P, HEADS], F32, mix)
        sink_in = sb("sink_in", [P, HEADS], F32, mix)
        sink_e = sb("sink_e", [P, HEADS], F32, mix)
        row_sum = sb("row_sum", [P, HEADS], F32, mix)
        row_inv = sb("row_inv", [P, HEADS], F32, mix)
        probs_flat = probs[:].rearrange("p h s -> p (h s)")
        q_rows = probs_flat[:, 0:T * SWA_W].rearrange("p (t c) -> p t c", t=T)
        span = 4 * (PAD + S)
        sums = [probs_flat[:, i * span:(i + 1) * span].rearrange("p (g s) -> p g s", g=4) for i in range(2)]
        means = probs_flat[:, 2 * span:2 * span + 4 * S].rearrange("p (g s) -> p g s", g=4)
        by_bank = lambda v: v[:].rearrange("p (b h) s -> p b (h s)", h=2)
        kmT_banks, qmT_banks, peer_qT = by_bank(kmT), by_bank(qmT), by_bank(scores_sb)
        mix.close()

        peer = ExitStack()
        rows = [sb(f"rows{i}", [P, D], F32, peer) for i in range(RING)]
        acc = sb("acc", [P, T, D], F32, peer)
        gain2 = sb("gain2", [P, 2, D], F32, peer)
        s12 = sb("s12", [P, 2 * PHEADS, KEYS], F32, peer)
        left = sb("left", [P, 2048], F32, peer)
        cand = sb("cand", [P, PHEADS, TOPK, TOPK], F32, peer)
        hit = sb("hit", [P, PHEADS, TOPK, TOPK], F32, peer)
        top_v = sb("top_v", [P, 2 * PHEADS, TOPK], F32, peer)
        top_i = sb("top_i", [P, 2 * PHEADS, TOPK], U32, peer)
        top_if = sb("top_if", [P, 2 * PHEADS, TOPK], F32, peer)
        best_v = sb("best_v", [P, PHEADS, TOPK], F32, peer)
        best_p = sb("best_p", [P, PHEADS, TOPK], U32, peer)
        digits = sb("digits", [P, 2, PHEADS, TOPK], U32, peer)
        digits_f = sb("digits_f", [P, 2, PHEADS, TOPK], F32, peer)
        chosen = sb("chosen", [P, 2, PHEADS, TOPK], F32, peer)
        experts = sb("experts", [P, T, PICKS], I32, peer)
        window = sb("window", [P, 2, TOPK], I32, peer)
        gate = sb("gate", [P, T, PHEADS, TOPK], F32, peer)
        gate_sum = sb("gate_sum", [P, PHEADS], F32, peer)
        hid = sb("hid", [P, T, PICKS], F32, peer)
        act_h = sb("act_h", [P, T, PICKS], F32, peer)
        weight = sb("weight", [P, T, PICKS], F32, peer)
        peer.close()

        x_in, mem_in, small_in, gain_in, gain2_in, out_done = (
            sem(n) for n in ("x_in", "mem_in", "small_in", "gain_in", "gain2_in", "out_done"))
        w_in_sem = [sem(f"w_in{i}") for i in range(RAW)]
        consts = sem("consts")
        turned = sem("turned")
        turned_hi = sem("turned_hi")
        turned_lo = sem("turned_lo")
        w_hi, w_lo, w_used = sem("w_hi"), sem("w_lo"), sem("w_used")
        evac = sem("evac")
        qk_turned, qk_out = sem("qk_turned"), sem("qk_out")
        dve_step = sem("dve_step")
        roped = sem("roped")
        sc_done, sc_read = sem("sc_done"), sem("sc_read")
        msc_done = sem("msc_done")
        max_ready, exp_done, probs_ready = sem("max_ready"), sem("exp_done"), sem("probs_ready")
        pt_done, pt_out, pv_done = sem("pt_done"), sem("pt_out"), sem("pv_done")
        heads_hi, heads_lo = sem("heads_hi"), sem("heads_lo")
        keys_turned, keys_out = sem("keys_turned"), sem("keys_out")
        pooled, pool_done = sem("pooled"), sem("pool_done")
        var_ready, std_ready, normed = sem("var_ready"), sem("std_ready"), sem("normed")
        s12_done, s12_out = sem("s12_done"), sem("s12_out")
        routed, gate_in, gate_e = sem("routed"), sem("gate_in"), sem("gate_e")
        window_set = sem("window_set")
        row_in = [sem(f"row_in{i}") for i in range(RING)]
        rows_used = sem("rows_used")
        gelu_done, acc_set = sem("gelu_done"), sem("acc_set")
        turns_ready, sines = sem("turns_ready"), sem("sines")

        n_evac = [0]
        for _, kinds in GROUPS:
            n_evac.append(n_evac[-1] + 2 * len(kinds))

        def unit_of(g, j):
            return UNITS * g + j

        block = ctx.enter_context(nc.Block())

        @block.sync
        def _(sp):
            sp.dma_start(resid[:], x[0].rearrange("(t p) d -> p t d", p=P)).then_inc(x_in, 16)
            sp.dma_start(scores_sb[:].rearrange("p h s -> p (h s)").rearrange("p (t d) -> p t d", t=T),
                         mem[0].rearrange("(t p) d -> p t d", p=P)).then_inc(mem_in, 16)

            def source(g, j):
                r0, r1 = j * PAIR * P, (j + 1) * PAIR * P
                name = GROUPS[g][0]

                def piece(w, c0, c1):
                    return w[0, r0:r1, c0:c1].rearrange("(a p) n -> p a n", p=P)
                if name == "q":
                    return [(0, piece(w_in, POOL_W, POOL_W + SWA_W))]
                if name == "kv":
                    return [(0, piece(w_in, POOL_W + SWA_W, POOL_W + SWA_W + 2 * KV_W))]
                if name == "mem":
                    return [(0, piece(w_mem_kv, 0, 2 * MEM_W))]
                if name == "pool_qm":
                    q0 = POOL_W + SWA_W + 2 * KV_W
                    return [(0, piece(w_in, 0, POOL_W)), (POOL_W, piece(w_in, q0, q0 + MEM_W))]
                w = w_out if name.startswith("out") else w_peer_q
                c0 = COLS * int(name[-1])
                return [(0, piece(w, c0, c0 + COLS))]

            counts = [0] * RAW
            for g in range(len(GROUPS)):
                for j in range(UNITS):
                    u = unit_of(g, j)
                    if u >= RAW:
                        sp.wait_ge(w_lo, u - RAW + 1)
                    for c0, src in source(g, j):
                        sp.dma_start(raw[:, u % RAW, :, c0:c0 + src.shape[2]], src).then_inc(w_in_sem[u % RAW], 16)
                if g == OUT0:
                    sp.wait_ge(pt_done, 16)
                    sp.dma_start(probs_flat[:, 0:D], ln1_g[0:1, :].to_broadcast([P, D])).then_inc(gain_in, 16)
                    sp.dma_start(probs_flat[:, D:2 * D], ln1_b[0:1, :].to_broadcast([P, D])).then_inc(gain_in, 16)
            sp.wait_ge(keys_out, 1)
            sp.dma_start(gain2[:, 0, :], ln2_g[0:1, :].to_broadcast([P, D])).then_inc(gain2_in, 16)
            sp.dma_start(gain2[:, 1, :], ln2_b[0:1, :].to_broadcast([P, D])).then_inc(gain2_in, 16)
            for t in range(T):
                sp.wait_ge(normed, T + t + 1)
                sp.dma_start(out[0, t * P:(t + 1) * P, :], acc[:, t, :]).then_inc(out_done, 16)
            sp.wait_ge(out_done, 16 * T)

        def pieces(g):
            return 2 if GROUPS[g][0] == "pool_qm" else 1

        def landed(u):
            n = 0
            for v in range(u % RAW, u + 1, RAW):
                n += 16 * pieces(v // UNITS)
            return n

        def width(g):
            return 512 * len(GROUPS[g][1])

        def q_heads(b):
            return ps[:, b, :].rearrange("p (m r c) -> p r m c", m=2, r=4)

        def q_pairs(b):
            return q_rows[:, b % 2, (b // 2) * 512:(b // 2 + 1) * 512].rearrange("p (r m c) -> p r m c", m=2, r=4)

        @block.gpsimd
        def _(pool):
            nc.gpsimd.memset(ident[:], 0.0).then_inc(consts, 1)
            nc.gpsimd.memset(mask[:], 0.0).then_inc(consts, 1)
            nc.gpsimd.memset(win_a[:], 0.0).then_inc(consts, 1)
            pool.wait_ge(consts, 3)
            nc.gpsimd.affine_select(out=ident[:], in_=ident[:], compare_op=ALU.not_equal, fill=1.0, base=0,
                                    pattern=[[-1, P]], channel_multiplier=1).then_inc(consts, 1)
            nc.gpsimd.affine_select(out=mask[:, 0, :], in_=mask[:, 0, :], compare_op=ALU.is_gt, fill=NEG, base=0,
                                    pattern=[[1, P]], channel_multiplier=-1).then_inc(consts, 1)
            nc.gpsimd.affine_select(out=mask[:, 1, :], in_=mask[:, 1, :], compare_op=ALU.is_ge, fill=NEG, base=0,
                                    pattern=[[-1, P]], channel_multiplier=1).then_inc(consts, 1)
            nc.gpsimd.iota(iota16[:], [[1, TOPK]], base=0, channel_multiplier=0,
                           allow_small_or_imprecise_dtypes=True).then_inc(consts, 1)
            nc.gpsimd.iota(inv_count[:], [[1, PAD]], base=1, channel_multiplier=0,
                           allow_small_or_imprecise_dtypes=True).then_inc(consts, 1)

            for phase in range(2 * T):
                t, table = phase // 2, (expert_u, expert_v)[phase % 2]
                first = phase * PICKS
                pool.wait_ge(routed, t + 1)
                with pool.Fori(0, PHEADS // 2) as i:
                    for half in range(2):
                        pool.wait_ge(rows_used, i * (2 * TOPK) + (first + half * TOPK + RING))
                        nc.gpsimd.tensor_copy(window[:, half, :],
                                              experts[:, t, bass.ds(i * (2 * TOPK) + half * TOPK, TOPK)]
                                              ).then_inc(window_set, 1)
                        pool.wait_ge(window_set, i * 2 + (phase * PHEADS + half + 1))
                        for k in range(TOPK):
                            pool.wait_ge(rows_used, i * (2 * TOPK) + (first + half * TOPK + k + 1 + TOPK))
                            pool.nop(nofuse=True)
                            nc.gpsimd.indirect_dma_start(
                                rows[k % RING][:], None, table[0],
                                bass.IndirectOffsetOnAxis(ap=window[:, half, k:k + 1], axis=0)
                            ).then_inc(row_in[k % RING], 16)

        @block.scalar
        def _(act):
            act.dma_start(pos_i[:], positions[0].rearrange("(t p) -> p t", p=P),
                          allow_slow_non_contiguous=True).then_inc(small_in, 16)
            act.dma_start(scale_sb[:], pool_scale[0].rearrange("(c p) -> p c", p=P),
                          allow_slow_non_contiguous=True).then_inc(small_in, 16)
            act.dma_start(sinks[:], attn_sinks[0:1, :].to_broadcast([P, HEADS])).then_inc(small_in, 16)
            act.dma_start(w_pool_sb[:], w_pool[0].rearrange("g c d -> c g d")).then_inc(small_in, 16)
            act.dma_start(keys_rows[:, 0, :], sub_keys_1[0]).then_inc(small_in, 16)
            act.dma_start(keys_rows[:, 1, :], sub_keys_2[0]).then_inc(small_in, 16)

            def turn_out(first, dst):
                for b in range(KC // 2):
                    act.wait_ge(turned, first + b + 1)
                    nc.scalar.activation(dst[:, 2 * b:2 * b + 2, :].rearrange("p a s -> p (a s)"),
                                         ps[:, 4 + (first + b) % 4, :], ACT.Copy).then_inc(turned_hi, 1)

            def split(g):
                for j in range(UNITS):
                    u = unit_of(g, j)
                    act.wait_ge(w_in_sem[u % RAW], landed(u))
                    if u >= SPLIT:
                        act.wait_ge(w_used, u - SPLIT + 1)
                    nc.scalar.activation(w_hi_sb[:, u % SPLIT, :, 0:width(g)], raw[:, u % RAW, :, 0:width(g)],
                                         ACT.Copy).then_inc(w_hi, 1)

            def read_out(g, banks, dst):
                act.wait_ge(w_used, unit_of(g, UNITS))
                for b in banks:
                    nc.scalar.activation(dst(b), ps[:, b, :], ACT.Copy).then_inc(evac, 1)

            turn_out(0, xT_hi)
            turn_out(8, yT_hi)
            act.wait_ge(turns_ready, 1)
            nc.scalar.activation(cossin[:], ang[:], ACT.Sin).then_inc(sines, 1)

            split(Q)
            for b in (0, 2):
                act.wait_ge(w_used, unit_of(Q, UNITS))
                nc.scalar.activation(q_pairs(b), q_heads(b), ACT.Copy).then_inc(evac, 1)
            split(KV)
            read_out(KV, (0,), lambda b: kv[:, b, :])
            split(MEM)
            read_out(MEM, (0, 2), lambda b: kmT_banks[:, b, :] if b < 2 else vm[:, b - 2, :])
            for i in range(5):
                act.wait_ge(qk_turned, i + 1)
                dst = qT[:, 2 * i:2 * i + 2, :] if i < 4 else kT[:]
                nc.scalar.activation(dst.rearrange("p a s -> p (a s)"), ps[:, 4 + i % 4, :], ACT.Copy
                                     ).then_inc(qk_out, 1)
            split(POOLQM)
            read_out(POOLQM, (2,), lambda b: qmT_banks[:, b - 2, :])

            act.wait_ge(pool_done, 1)
            for g in range(4):
                nc.scalar.activation(yT_hi[:, g, :], ps[:, g // 2, (g % 2) * S:(g % 2 + 1) * S], ACT.Copy,
                                     scale=scale_sb[:, g:g + 1]).then_inc(heads_hi, 1)

            def pt_copy(f):
                act.wait_ge(pt_done, f + 1)
                if f >= 2:
                    act.wait_ge(pv_done, f - 1)
                nc.scalar.activation(pT[:, f % 2, :], ps[:, 4 + f % 2, :], ACT.Copy).then_inc(pt_out, 1)

            f = 0
            for t in range(T):
                nk = P * (t + 1)
                act.wait_ge(max_ready, t + 1)
                for h in range(HEADS):
                    last = nc.scalar.activation(probs[:, h, 0:nk], scores_sb[:, h, 0:nk], ACT.Exp,
                                                bias=neg_max[:, h:h + 1], accum_out=row_sum[:, h:h + 1])
                last = nc.scalar.activation(sink_e[:], sink_in[:], ACT.Exp)
                last.then_inc(exp_done, 1)
                for _ in range(4 * (t + 1)):
                    pt_copy(f)
                    f += 1
                act.wait_ge(pv_done, f)
                for b in range(2):
                    nc.scalar.activation(yT_hi[:, 4 + 4 * b:8 + 4 * b, t * P:(t + 1) * P],
                                         ps[:, 6 + b, :].rearrange("p (c s) -> p c s", c=4), ACT.Copy
                                         ).then_inc(heads_hi, 1)
            act.wait_ge(max_ready, T + 1)
            for n in range(T * MHEADS):
                last = nc.scalar.activation(probs[:, n, :], ps[:, n // 2, (n % 2) * S:(n % 2 + 1) * S], ACT.Exp,
                                            bias=neg_max[:, n:n + 1], scale=float(MHD) ** -0.5,
                                            accum_out=row_sum[:, n:n + 1])
            last.then_inc(exp_done, 1)
            for _ in range(4):
                pt_copy(f)
                f += 1
            act.wait_ge(pv_done, f)
            for t in range(T):
                nc.scalar.activation(yT_hi[:, 12:16, t * P:(t + 1) * P],
                                     ps[:, 6 + t, :].rearrange("p (c s) -> p c s", c=4), ACT.Copy
                                     ).then_inc(heads_hi, 1)
            split(OUT0)
            split(OUT1)
            for t in range(T):
                act.wait_ge(var_ready, t + 1)
                nc.scalar.activation(rstd[:, t, 0:1], rstd[:, t, 1:2], ACT.Sqrt).then_inc(std_ready, 1)
            turn_out(16, xT_hi)
            split(PEER0)
            read_out(PEER0, (0, 2), lambda b: peer_qT[:, b, :])
            split(PEER1)
            read_out(PEER1, (0, 2), lambda b: peer_qT[:, 4 + b, :])

            act.wait_ge(keys_turned, 1)
            nc.scalar.activation(keysT[:].rearrange("p a k -> p (a k)"), ps[:, 4, 0:2 * KEYS], ACT.Copy
                                 ).then_inc(keys_out, 1)

            def route(t):
                for b in range(4):
                    act.wait_ge(s12_done, 4 * t + b + 1)
                    if t and b == 0:
                        act.wait_ge(routed, t)
                    nc.scalar.activation(s12[:, 4 * b:4 * b + 4, :].rearrange("p a s -> p (a s)"),
                                         ps[:, 4 * (1 - t) + b, :], ACT.Copy).then_inc(s12_out, 1)
                act.wait_ge(gate_in, t + 1)
                nc.scalar.activation(gate[:, t], gate[:, t], ACT.Exp).then_inc(gate_e, 1)

            def gelu(t):
                act.wait_ge(rows_used, PRESET + (2 * t + 1) * PICKS)
                nc.scalar.activation(act_h[:, t, :], hid[:, t, :], ACT.Gelu).then_inc(gelu_done, 1)

            route(0)
            for t in range(T):
                nc.scalar.activation(acc[:, t, :], resid[:, t, :], ACT.Copy, scale=ALPHA).then_inc(acc_set, 1)
            gelu(0)
            route(1)
            for t in range(T):
                if t:
                    gelu(t)
                act.wait_ge(var_ready, T + t + 1)
                nc.scalar.activation(rstd[:, t, 0:1], rstd[:, t, 1:2], ACT.Sqrt).then_inc(std_ready, 1)

        @block.vector
        def _(dve):
            steps = [0]

            def link(ins):
                steps[0] += 1
                ins.then_inc(dve_step, 1)
                dve.wait_ge(dve_step, steps[0])

            def turn_low(first, hi, lo):
                for b in range(KC // 2):
                    dve.wait_ge(turned_hi, first + b + 1)
                    nc.vector.tensor_tensor(lo[:, 2 * b:2 * b + 2, :].rearrange("p a s -> p (a s)"),
                                            ps[:, 4 + (first + b) % 4, :],
                                            hi[:, 2 * b:2 * b + 2, :].rearrange("p a s -> p (a s)").bitcast(F32),
                                            ALU.subtract).then_inc(turned_lo, 1)

            def split(g):
                for j in range(UNITS):
                    u = unit_of(g, j)
                    dve.wait_ge(w_hi, u + 1)
                    nc.vector.tensor_tensor(w_lo_sb[:, u % SPLIT, :, 0:width(g)], raw[:, u % RAW, :, 0:width(g)],
                                            w_hi_sb[:, u % SPLIT, :, 0:width(g)].bitcast(F32),
                                            ALU.subtract).then_inc(w_lo, 1)

            def read_out(g, banks, dst):
                dve.wait_ge(w_used, unit_of(g, UNITS))
                for b in banks:
                    nc.vector.tensor_copy(dst(b), ps[:, b, :]).then_inc(evac, 1)

            dve.wait_ge(small_in, 16 * 6)
            link(nc.vector.tensor_copy(pos_f[:], pos_i[:]))
            for j in range(HALF):
                last = nc.vector.tensor_scalar(ang[:, 1, :, j], pos_f[:], float(THETA ** (-2.0 * j / ROPE)), None,
                                               ALU.mult)
            link(last)
            link(nc.vector.tensor_scalar(ang[:, 0], ang[:, 1], PI / 2, None, ALU.add))
            link(nc.vector.tensor_scalar(turns[:], ang[:], 0.5 / PI, ROUND, ALU.mult, ALU.add))
            link(nc.vector.tensor_scalar(turns[:], turns[:], ROUND, None, ALU.subtract))
            for part in TWO_PI:
                link(nc.vector.scalar_tensor_tensor(out=ang[:], in0=turns[:], scalar=-part, in1=ang[:],
                                                    op0=ALU.mult, op1=ALU.add))
            nc.vector.tensor_scalar(ang[:], ang[:], -3.1415925, 3.1415925, ALU.max, ALU.min
                                    ).then_inc(turns_ready, 1)
            dve.wait_ge(consts, 8)
            link(nc.vector.reciprocal(inv_count[:], inv_count[:]))

            turn_low(0, xT_hi, xT_lo)
            turn_low(8, yT_hi, yT_lo)
            split(Q)
            for b in (1, 3):
                dve.wait_ge(w_used, unit_of(Q, UNITS))
                nc.vector.tensor_copy(q_pairs(b), q_heads(b)).then_inc(evac, 1)
            split(KV)
            read_out(KV, (1,), lambda b: kv[:, b, :])
            dve.wait_ge(sines, 1)
            dve.wait_ge(evac, n_evac[KV + 1])
            turned_rows = 0
            for t in range(T):
                for rows_, n in ((q_rows[:, t, :], HEADS), (kv[:, t, 0:KV_W], KV_W // HD)):
                    heads = rows_.rearrange("p (h c) -> p h c", c=HD)
                    a, b = heads[:, :, 0:HALF], heads[:, :, HALF:ROPE]
                    cos = cossin[:, 0, t, :].unsqueeze(1).to_broadcast([P, n, HALF])
                    sin = cossin[:, 1, t, :].unsqueeze(1).to_broadcast([P, n, HALF])
                    r = [rt[:, k, 0:n * HALF].rearrange("p (h c) -> p h c", c=HALF) for k in range(4)]
                    nc.vector.tensor_tensor(r[0], a, cos, ALU.mult)
                    nc.vector.tensor_tensor(r[1], b, sin, ALU.mult)
                    nc.vector.tensor_tensor(r[2], b, cos, ALU.mult)
                    link(nc.vector.tensor_tensor(r[3], a, sin, ALU.mult))
                    nc.vector.tensor_tensor(a, r[0], r[1], ALU.subtract)
                    nc.vector.tensor_tensor(b, r[2], r[3], ALU.add).then_inc(roped, 1)
                    turned_rows += 1
                    dve.wait_ge(roped, turned_rows)
            split(MEM)
            read_out(MEM, (1, 3), lambda b: kmT_banks[:, b, :] if b < 2 else vm[:, b - 2, :])
            split(POOLQM)
            read_out(POOLQM, (3,), lambda b: qmT_banks[:, b - 2, :])
            for b in (0, 1):
                last = nc.vector.tensor_copy(win_a[:, 2 * b:2 * b + 2, PAD:],
                                             ps[:, b, :].rearrange("p (g s) -> p g s", g=2))
                last.then_inc(evac, 1)

            dve.wait_ge(evac, n_evac[POOLQM + 1])
            dve.wait_ge(qk_turned, 4)
            for dst in sums:
                last = nc.vector.memset(dst[:, :, 0:PAD], 0.0)
            link(last)
            src = win_a
            for lev in range(4):
                dst, back, w = sums[lev % 2], 1 << lev, WINDOWS[lev]
                nc.vector.tensor_scalar(edge[:, 0:w], inv_count[:, 0:w], float(w), None, ALU.mult)
                link(nc.vector.tensor_tensor(dst[:, lev:4, PAD:], src[:, lev:4, PAD:],
                                             src[:, lev:4, PAD - back:PAD + S - back], ALU.add))
                link(nc.vector.tensor_tensor(dst[:, lev, PAD:PAD + w], dst[:, lev, PAD:PAD + w], edge[:, 0:w],
                                             ALU.mult))
                nc.vector.scalar_tensor_tensor(out=means[:, lev, :], in0=dst[:, lev, PAD:], scalar=1.0 / w,
                                               in1=win_a[:, lev, PAD:], op0=ALU.mult, op1=ALU.subtract
                                               ).then_inc(pooled, 1)
                dve.wait_ge(pooled, lev + 1)
                src = dst
            for g in range(4):
                dve.wait_ge(heads_hi, 2 * (g // 2) + 2)
                nc.vector.scalar_tensor_tensor(out=yT_lo[:, g, :], in0=ps[:, g // 2, (g % 2) * S:(g % 2 + 1) * S],
                                               scalar=scale_sb[:, g:g + 1], in1=yT_hi[:, g, :].bitcast(F32),
                                               op0=ALU.mult, op1=ALU.subtract).then_inc(heads_lo, 1)

            for t in range(T):
                nk = P * (t + 1)
                for p in range(4):
                    dve.wait_ge(sc_done, 4 * t + p + 1)
                    if t and p == 0:
                        dve.wait_ge(exp_done, t)
                    for m in range(2):
                        h0 = 8 * (p // 2) + 4 * m + 2 * (p % 2)
                        sc = ps[:, 2 * (p % 2) + m, 0:2 * nk].rearrange("p (h s) -> p h s", h=2)
                        mk = mask[:, 1 - t:2, :].rearrange("p a s -> p (a s)").unsqueeze(1).to_broadcast([P, 2, nk])
                        last = nc.vector.scalar_tensor_tensor(out=scores_sb[:, h0:h0 + 2, 0:nk], in0=sc,
                                                              scalar=float(HD) ** -0.5, in1=mk,
                                                              op0=ALU.mult, op1=ALU.add)
                        last.then_inc(sc_read, 1)
                dve.wait_ge(sc_read, 8 * (t + 1))
                link(nc.vector.reduce_max(row_max[:], scores_sb[:, :, 0:nk], AX.X))
                link(nc.vector.tensor_tensor(row_max[:], row_max[:], sinks[:], ALU.max))
                nc.vector.tensor_scalar(neg_max[:], row_max[:], -1.0, None, ALU.mult)
                nc.vector.tensor_tensor(sink_in[:], sinks[:], row_max[:], ALU.subtract).then_inc(max_ready, 1)
                dve.wait_ge(exp_done, t + 1)
                link(nc.vector.tensor_tensor(row_sum[:], row_sum[:], sink_e[:], ALU.add))
                link(nc.vector.reciprocal(row_inv[:], row_sum[:]))
                nc.vector.tensor_tensor(probs[:, :, 0:nk], probs[:, :, 0:nk],
                                        row_inv[:].unsqueeze(2).to_broadcast([P, HEADS, nk]), ALU.mult
                                        ).then_inc(probs_ready, 1)
                for b in range(2):
                    dve.wait_ge(heads_hi, 4 + 2 * t + b + 1)
                    nc.vector.tensor_tensor(yT_lo[:, 4 + 4 * b:8 + 4 * b, t * P:(t + 1) * P],
                                            ps[:, 6 + b, :].rearrange("p (c s) -> p c s", c=4),
                                            yT_hi[:, 4 + 4 * b:8 + 4 * b, t * P:(t + 1) * P].bitcast(F32),
                                            ALU.subtract).then_inc(heads_lo, 1)
            for b in range(4):
                dve.wait_ge(msc_done, b + 1)
                last = nc.vector.reduce_max(row_max[:, 2 * b:2 * b + 2],
                                            ps[:, b, :].rearrange("p (h s) -> p h s", h=2), AX.X)
            link(last)
            nc.vector.tensor_scalar(neg_max[:, 0:8], row_max[:, 0:8], -float(MHD) ** -0.5, None, ALU.mult
                                    ).then_inc(max_ready, 1)
            dve.wait_ge(exp_done, T + 1)
            link(nc.vector.reciprocal(row_inv[:, 0:8], row_sum[:, 0:8]))
            nc.vector.tensor_tensor(probs[:, 0:8, :], probs[:, 0:8, :],
                                    row_inv[:, 0:8].unsqueeze(2).to_broadcast([P, 8, S]), ALU.mult
                                    ).then_inc(probs_ready, 1)
            for t in range(T):
                dve.wait_ge(heads_hi, 4 + 2 * T + t + 1)
                nc.vector.tensor_tensor(yT_lo[:, 12:16, t * P:(t + 1) * P],
                                        ps[:, 6 + t, :].rearrange("p (c s) -> p c s", c=4),
                                        yT_hi[:, 12:16, t * P:(t + 1) * P].bitcast(F32),
                                        ALU.subtract).then_inc(heads_lo, 1)

            for g in (OUT0, OUT1):
                split(g)
                dve.wait_ge(w_used, unit_of(g, UNITS))
                for b in range(4):
                    c0 = COLS * (g - OUT0) + 512 * (b // 2)
                    cols = resid[:, b % 2, c0:c0 + 512]
                    nc.vector.scalar_tensor_tensor(out=cols, in0=cols, scalar=ALPHA, in1=ps[:, b, :],
                                                   op0=ALU.mult, op1=ALU.add).then_inc(evac, 1)

            def norm(tile, t, n, gain, shift):
                for c in range(4):
                    last = nc.vector.bn_stats(stats[:, t, c, :], tile[:, 512 * c:512 * (c + 1)])
                link(last)
                link(nc.vector.bn_aggr(moments[:, t, :], stats[:, t].rearrange("p c k -> p (c k)")))
                nc.vector.tensor_scalar(rstd[:, t, 1:2], moments[:, t, 1:2], EPS, None, ALU.add
                                        ).then_inc(var_ready, 1)
                dve.wait_ge(std_ready, n + 1)
                link(nc.vector.reciprocal(rstd[:, t, 2:3], rstd[:, t, 0:1]))
                link(nc.vector.tensor_tensor(rstd[:, t, 3:4], rstd[:, t, 2:3], rstd[:, t, 2:3], ALU.mult))
                link(nc.vector.tensor_tensor(rstd[:, t, 3:4], rstd[:, t, 3:4], rstd[:, t, 1:2], ALU.mult))
                link(nc.vector.tensor_scalar(rstd[:, t, 3:4], rstd[:, t, 3:4], -0.5, 1.5, ALU.mult, ALU.add))
                link(nc.vector.tensor_tensor(rstd[:, t, 2:3], rstd[:, t, 2:3], rstd[:, t, 3:4], ALU.mult))
                link(nc.vector.tensor_scalar(tile, tile, moments[:, t, 0:1], rstd[:, t, 2:3],
                                             ALU.subtract, ALU.mult))
                link(nc.vector.tensor_tensor(tile, tile, gain, ALU.mult))
                nc.vector.tensor_tensor(tile, tile, shift, ALU.add).then_inc(normed, 1)

            dve.wait_ge(evac, n_evac[OUT1 + 1])
            dve.wait_ge(gain_in, 32)
            for t in range(T):
                norm(resid[:, t, :], t, t, probs_flat[:, 0:D], probs_flat[:, D:2 * D])
            turn_low(16, xT_hi, xT_lo)
            split(PEER0)
            read_out(PEER0, (1, 3), lambda b: peer_qT[:, b, :])
            split(PEER1)
            read_out(PEER1, (1, 3), lambda b: peer_qT[:, 4 + b, :])
            dve.sem_inc(rows_used, PRESET)

            def top16(n, values, rest, best, index):
                for r in range(n):
                    last = nc.vector.max(best(r)[:, 0:8], values(r))
                link(last)
                for r in range(n):
                    last = nc.vector.match_replace(rest(r), best(r)[:, 0:8], values(r), LOWEST)
                link(last)
                for r in range(n):
                    last = nc.vector.max(best(r)[:, 8:16], rest(r))
                link(last)
                for r in range(n):
                    nc.vector.max_index(index(r)[:, 0:8], best(r)[:, 0:8], values(r))
                    last = nc.vector.max_index(index(r)[:, 8:16], best(r)[:, 8:16], rest(r))
                link(last)

            def route(t):
                dve.wait_ge(s12_out, 4 * (t + 1))
                left3 = left[:].rearrange("p (r k) -> p r k", k=KEYS)
                top16(2 * PHEADS, lambda r: s12[:, r, :], lambda r: left3[:, r, :],
                      lambda r: top_v[:, r, :], lambda r: top_i[:, r, :])
                nc.vector.tensor_copy(top_if[:], top_i[:])
                tv = top_v[:].rearrange("p (h a) k -> p h a k", a=2)
                link(nc.vector.tensor_tensor(
                    cand[:], tv[:, :, 0, :].unsqueeze(3).to_broadcast([P, PHEADS, TOPK, TOPK]),
                    tv[:, :, 1, :].unsqueeze(2).to_broadcast([P, PHEADS, TOPK, TOPK]), ALU.add))
                left4 = left[:].rearrange("p (h k) -> p h k", k=TOPK * TOPK)
                top16(PHEADS, lambda h: cand[:, h].rearrange("p a b -> p (a b)"), lambda h: left4[:, h, :],
                      lambda h: best_v[:, h, :], lambda h: best_p[:, h, :])
                nc.vector.tensor_tensor(gate[:, t], best_v[:], best_v[:, :, 0:1].to_broadcast([P, PHEADS, TOPK]),
                                        ALU.subtract).then_inc(gate_in, 1)
                nc.vector.tensor_scalar(digits[:, 0], best_p[:], 4, None, ALU.logical_shift_right)
                link(nc.vector.tensor_scalar(digits[:, 1], best_p[:], TOPK - 1, None, ALU.bitwise_and))
                link(nc.vector.tensor_copy(digits_f[:], digits[:]))
                tif = top_if[:].rearrange("p (h a) k -> p h a k", a=2)
                for a in range(2):
                    link(nc.vector.tensor_tensor(
                        hit[:], digits_f[:, a].unsqueeze(3).to_broadcast([P, PHEADS, TOPK, TOPK]),
                        iota16[:].unsqueeze(1).unsqueeze(1).to_broadcast([P, PHEADS, TOPK, TOPK]), ALU.is_equal))
                    link(nc.vector.tensor_tensor(
                        hit[:], hit[:], tif[:, :, a, :].unsqueeze(2).to_broadcast([P, PHEADS, TOPK, TOPK]), ALU.mult))
                    link(nc.vector.reduce_sum(chosen[:, a], hit[:], AX.X))
                nc.vector.scalar_tensor_tensor(out=experts[:, t, :], in0=chosen[:, 0].rearrange("p h k -> p (h k)"),
                                               scalar=float(KEYS), in1=chosen[:, 1].rearrange("p h k -> p (h k)"),
                                               op0=ALU.mult, op1=ALU.add).then_inc(routed, 1)
                dve.wait_ge(gate_e, t + 1)
                link(nc.vector.reduce_sum(gate_sum[:], gate[:, t], AX.X))
                link(nc.vector.reciprocal(gate_sum[:], gate_sum[:]))
                link(nc.vector.tensor_tensor(gate[:, t], gate[:, t],
                                             gate_sum[:].unsqueeze(2).to_broadcast([P, PHEADS, TOPK]), ALU.mult))

            def gathered(i, first, k):
                dve.wait_ge(row_in[k % RING], i * (16 * TOPK // RING) + 16 * ((first + k) // RING + 1))

            route(0)
            for t in range(T):
                first = 2 * t * PICKS
                with dve.Fori(0, PHEADS) as i:
                    for k in range(TOPK):
                        gathered(i, first, k)
                        nc.vector.scalar_tensor_tensor(
                            out=rows[k % RING][:], in0=rows[k % RING][:], scalar=1.0, in1=resid[:, t, :],
                            op0=ALU.mult, op1=ALU.mult,
                            accum_out=hid[:, t, bass.ds(i * TOPK + k, 1)]).then_inc(rows_used, 1)
                if t == 0:
                    route(1)
                dve.wait_ge(gelu_done, t + 1)
                link(nc.vector.tensor_tensor(weight[:, t, :], act_h[:, t, :], gate[:, t].rearrange("p h k -> p (h k)"),
                                             ALU.mult))
                first += PICKS
                dve.wait_ge(acc_set, T)
                with dve.Fori(0, PHEADS) as i:
                    for k in range(TOPK):
                        gathered(i, first, k)
                        dve.wait_ge(rows_used, i * TOPK + (first + k + PRESET))
                        nc.vector.scalar_tensor_tensor(
                            out=acc[:, t, :], in0=rows[k % RING][:], scalar=weight[:, t, bass.ds(i * TOPK + k, 1)],
                            in1=acc[:, t, :], op0=ALU.mult, op1=ALU.add).then_inc(rows_used, 1)
                dve.wait_ge(rows_used, PRESET + first + PICKS)
                dve.wait_ge(gain2_in, 32)
                norm(acc[:, t, :], t, T + t, gain2[:, 0, :], gain2[:, 1, :])

        @block.tensor
        def _(pe):
            def turn(first, src):
                for b in range(KC // 2):
                    if first + b >= 4:
                        pe.wait_ge(turned_lo, first + b - 3)
                    for c in range(2):
                        for t in range(T):
                            k = 2 * b + c
                            last = nc.tensor.transpose(ps[:, 4 + (first + b) % 4, (2 * c + t) * P:(2 * c + t + 1) * P],
                                                       src(t)[:, k * P:(k + 1) * P], ident[:])
                    last.then_inc(turned, 1)

            def group(g, hi, lo):
                if g:
                    pe.wait_ge(evac, n_evac[g])
                for j in range(UNITS):
                    u = unit_of(g, j)
                    pe.wait_ge(w_lo, u + 1)
                    for a in range(PAIR):
                        k = PAIR * j + a
                        first, final = k == 0, k == KC - 1
                        for half, kind in enumerate(GROUPS[g][1]):
                            wh = w_hi_sb[:, u % SPLIT, a, 512 * half:512 * half + 512]
                            wl = w_lo_sb[:, u % SPLIT, a, 512 * half:512 * half + 512]
                            if kind == "R":
                                for t in range(T):
                                    o = ps[:, 2 * half + t, :]
                                    xh, xl = (v[:, k, t * P:(t + 1) * P] for v in (hi, lo))
                                    nc.tensor.matmul(o, xh, wh, start=first, stop=False)
                                    nc.tensor.matmul(o, xh, wl, start=False, stop=False)
                                    last = nc.tensor.matmul(o, xl, wh, start=False, stop=final)
                            else:
                                for b in range(4):
                                    o = ps[:, 2 * half + b // 2, (b % 2) * S:(b % 2 + 1) * S]
                                    wbh, wbl = wh[:, b * P:(b + 1) * P], wl[:, b * P:(b + 1) * P]
                                    nc.tensor.matmul(o, wbh, hi[:, k, :], start=first and b % 2 == 0, stop=False,
                                                     skip_group_check=True)
                                    nc.tensor.matmul(o, wbh, lo[:, k, :], start=False, stop=False,
                                                     skip_group_check=True)
                                    last = nc.tensor.matmul(o, wbl, hi[:, k, :], start=False, stop=final,
                                                            skip_group_check=True)
                    last.then_inc(w_used, 1)

            pe.wait_ge(consts, 4)
            pe.wait_ge(x_in, 16)
            turn(0, lambda t: resid[:, t, :])
            pe.wait_ge(mem_in, 16)
            mem_rows = scores_sb[:].rearrange("p h s -> p (h s)")
            turn(8, lambda t: mem_rows[:, t * D:(t + 1) * D])
            pe.wait_ge(turned_lo, 16)
            group(Q, xT_hi, xT_lo)
            group(KV, xT_hi, xT_lo)
            group(MEM, yT_hi, yT_lo)
            pe.wait_ge(roped, 2 * T)
            for i in range(5):
                if i == 4:
                    pe.wait_ge(qk_out, 1)
                for c in range(2):
                    for t in range(T):
                        j = 2 * i + c
                        src = q_rows[:, t, j * P:(j + 1) * P] if i < 4 else kv[:, t, c * P:(c + 1) * P]
                        last = nc.tensor.transpose(ps[:, 4 + i % 4, (2 * c + t) * P:(2 * c + t + 1) * P], src, ident[:])
                last.then_inc(qk_turned, 1)
            group(POOLQM, xT_hi, xT_lo)
            pe.wait_ge(evac, n_evac[POOLQM + 1])
            pe.wait_ge(pooled, 4)
            for g in range(4):
                last = nc.tensor.matmul(ps[:, g // 2, (g % 2) * S:(g % 2 + 1) * S], w_pool_sb[:, g, :],
                                        means[:, g, :], start=True, stop=True)
            last.then_inc(pool_done, 1)
            pe.wait_ge(heads_lo, 4)
            pe.wait_ge(qk_out, 5)

            f = 0
            for t in range(T):
                nk = P * (t + 1)
                for p in range(4):
                    n = 4 * t + p
                    if n >= 2:
                        pe.wait_ge(sc_read, 2 * (n - 1))
                    g = p // 2
                    for m in range(2):
                        for r in range(2):
                            j = 4 * g + 2 * (p % 2) + r
                            last = nc.tensor.matmul(ps[:, 2 * (p % 2) + m, r * nk:(r + 1) * nk],
                                                    qT[64 * m:64 * m + 64, j, t * P:(t + 1) * P],
                                                    kT[64 * m:64 * m + 64, g, 0:nk], start=True, stop=True)
                    last.then_inc(sc_done, 1)
                pe.wait_ge(probs_ready, t + 1)
                if t:
                    pe.wait_ge(heads_lo, 4 + 2 * t)

                def weigh(n, f0):
                    pe.wait_ge(pt_out, f0 + n + 1)
                    slot = (f0 + n) % 2
                    for i in range(4 // (t + 1)):
                        h = n * (4 // (t + 1)) + i
                        o = ps[64 * (h % 2):64 * (h % 2) + 64, 6 + h // 8, (h // 2 % 4) * P:(h // 2 % 4 + 1) * P]
                        for c in range(t + 1):
                            last = nc.tensor.matmul(o, kv[:, c, KV_W + HD * (h // 4):KV_W + HD * (h // 4 + 1)],
                                                    pT[:, slot, (i * (t + 1) + c) * P:(i * (t + 1) + c + 1) * P],
                                                    start=(c == 0), stop=(c == t))
                    last.then_inc(pv_done, 1)

                banks = 4 * (t + 1)
                f0 = f
                for n in range(banks):
                    if f >= 2:
                        pe.wait_ge(pt_out, f - 1)
                    for i in range(4):
                        h, c = (4 * n + i, 0) if t == 0 else (2 * n + i // 2, i % 2)
                        last = nc.tensor.transpose(ps[:, 4 + f % 2, i * P:(i + 1) * P],
                                                   probs[:, h, c * P:(c + 1) * P], ident[:])
                    last.then_inc(pt_done, 1)
                    f += 1
                    if n:
                        weigh(n - 1, f0)
                weigh(banks - 1, f0)

            pe.wait_ge(sc_read, 16)
            for b in range(4):
                for i in range(2):
                    t, h = b // 2, 2 * (b % 2) + i
                    last = nc.tensor.matmul(ps[:, b, i * S:(i + 1) * S], qmT[:, h, t * P:(t + 1) * P], kmT[:, h, :],
                                            start=True, stop=True)
                last.then_inc(msc_done, 1)
            pe.wait_ge(probs_ready, T + 1)
            pe.wait_ge(heads_lo, 4 + 2 * T)

            def weigh_mem(n, f0):
                pe.wait_ge(pt_out, f0 + n + 1)
                slot = (f0 + n) % 2
                for i in range(2):
                    t, h = n // 2, 2 * (n % 2) + i
                    for c in range(2):
                        last = nc.tensor.matmul(ps[:, 6 + t, h * P:(h + 1) * P], vm[:, c, h * MHD:(h + 1) * MHD],
                                                pT[:, slot, (2 * i + c) * P:(2 * i + c + 1) * P],
                                                start=(c == 0), stop=(c == 1))
                last.then_inc(pv_done, 1)

            f0 = f
            for n in range(4):
                pe.wait_ge(pt_out, f - 1)
                for i in range(4):
                    last = nc.tensor.transpose(ps[:, 4 + f % 2, i * P:(i + 1) * P],
                                               probs[:, 2 * n + i // 2, (i % 2) * P:(i % 2 + 1) * P], ident[:])
                last.then_inc(pt_done, 1)
                f += 1
                if n:
                    weigh_mem(n - 1, f0)
            weigh_mem(3, f0)

            pe.wait_ge(heads_lo, 3 * T + 4)
            group(OUT0, yT_hi, yT_lo)
            group(OUT1, yT_hi, yT_lo)
            pe.wait_ge(normed, T)
            turn(16, lambda t: resid[:, t, :])
            pe.wait_ge(turned_lo, 24)
            group(PEER0, xT_hi, xT_lo)
            group(PEER1, xT_hi, xT_lo)
            for a in range(2):
                last = nc.tensor.transpose(ps[:, 4, a * P:(a + 1) * P], keys_rows[:, a, :], ident[:])
            last.then_inc(keys_turned, 1)
            pe.wait_ge(evac, n_evac[PEER1 + 1])
            pe.wait_ge(keys_out, 1)
            scT = scores_sb[:]
            for t in range(T):
                for b in range(4):
                    for i in range(4):
                        r = 4 * b + i
                        last = nc.tensor.matmul(ps[:, 4 * (1 - t) + b, i * P:(i + 1) * P],
                                                scT[:, r, t * P:(t + 1) * P], keysT[:, r % 2, :],
                                                start=True, stop=True)
                    last.then_inc(s12_done, 1)


_INS = ["x", "mem", "positions", "w_in", "w_mem_kv", "w_pool", "pool_scale", "attn_sinks", "w_out", "ln1_g", "ln1_b",
        "w_peer_q", "sub_keys_1", "sub_keys_2", "expert_u", "expert_v", "ln2_g", "ln2_b"]


def kernel(**inputs):
    import numpy as np
    import concourse.bacc as bacc
    from concourse.bass_utils import run_bass_kernel_spmd

    nc = bacc.Bacc("TRN2", target_bir_lowering=False, num_devices=1)
    arrays, args = {}, []
    for name in _INS:
        a = np.ascontiguousarray(inputs[name])
        arrays[name] = a
        args.append(nc.dram_tensor(name, a.shape, mybir.dt.from_np(a.dtype), kind="ExternalInput").ap())
    args.append(nc.dram_tensor("out", (1, S, D), F32, kind="ExternalOutput").ap())
    hybrid_layer(nc, *args)
    got = run_bass_kernel_spmd(nc, [arrays], core_ids=[0])
    return got.results[0]["out"]
```

```python
import concourse.bass as bass
from concourse import mybir
from contextlib import ExitStack

F32 = mybir.dt.float32
F32R = mybir.dt.float32r
I32 = mybir.dt.int32
U32 = mybir.dt.uint32
ALU = mybir.AluOpType
ACT = mybir.ActivationFunctionType
AX = mybir.AxisListType

P = 128
D = 2048
S = 256
T = S // P
KC = D // P
POOL_W, SWA_W, KV_W, MEM_W = 512, 1024, 256, 512
WINDOWS = (2, 4, 8, 16)
PAD = WINDOWS[-1]
HEADS, HD = 16, 64
MHEADS, MHD = 4, 128
ROPE = HD // 4
HALF = ROPE // 2
THETA = 500000.0
PHEADS, KEYS, TOPK = 8, 128, 16
PICKS = PHEADS * TOPK
ALPHA = 2.0 ** 0.25
EPS = 1e-5
NEG = -1e30
LOWEST = -3.0e38
PI = 3.14159265358979
ROUND = 12582912.0
TWO_PI = (6.28125, 0.0019350051879882812, 3.0199159819e-07)

COLS = 1024
PAIR = 2
UNITS = KC // PAIR
RAW = 2
SPLIT = 2
RING = 4
PRESET = RING + TOPK
STEPS = 4
STEP_H = PHEADS // STEPS

CH = 512
DCH = 3
DENSE = DCH * CH
TAIL = D - DENSE
BLOCKS = KEYS
VRAW = 4
VSPLIT = 4
VRING = 4
VPRESET = 2 * VRING
ONES = 16

GROUPS = (
    ("q", "RR"),
    ("kv", "R"),
    ("mem", "TR"),
    ("pool_qm", "TT"),
    ("out0", "RR"),
    ("out1", "RR"),
    ("peer0", "TT"),
    ("peer1", "TT"),
)
Q, KV, MEM, POOLQM, OUT0, OUT1, PEER0, PEER1 = range(len(GROUPS))


def hybrid_layer(nc, x, mem, positions, w_in, w_mem_kv, w_pool, pool_scale, attn_sinks, w_out, ln1_g, ln1_b,
                 w_peer_q, sub_keys_1, sub_keys_2, expert_u, expert_v, ln2_g, ln2_b, out):
    ctx = ExitStack()
    with ctx:
        def sb(name, shape, dt, where=ctx):
            return where.enter_context(nc.sbuf_tensor(name, shape, dt))

        def sem(name):
            return ctx.enter_context(nc.semaphore(name))

        resid = sb("resid", [P, T, D], F32)
        ident = sb("ident", [P, P], F32)
        keysT = sb("keysT", [P, 2, KEYS], F32)
        stats = sb("stats", [P, T, 4, 6], F32)
        moments = sb("moments", [P, T, 2], F32)
        rstd = sb("rstd", [P, T, 4], F32)
        iota = sb("iota", [P, KEYS], F32)
        ps = ctx.enter_context(nc.psum_tensor("ps", [P, 8, 512], F32))

        mix = ExitStack()
        probs = sb("probs", [P, HEADS, S], F32, mix)
        yT_hi = sb("yT_hi", [P, KC, S], F32R, mix)
        yT_lo = sb("yT_lo", [P, KC, S], F32R, mix)
        xT_hi = sb("xT_hi", [P, KC, S], F32R, mix)
        xT_lo = sb("xT_lo", [P, KC, S], F32R, mix)
        raw = sb("raw", [P, RAW, PAIR, COLS], F32, mix)
        w_hi_sb = sb("w_hi_sb", [P, SPLIT, PAIR, COLS], F32R, mix)
        w_lo_sb = sb("w_lo_sb", [P, SPLIT, PAIR, COLS], F32R, mix)
        scores_sb = sb("scores_sb", [P, HEADS, S], F32, mix)
        kv = sb("kv", [P, T, 2 * KV_W], F32, mix)
        qT = sb("qT", [P, HEADS // 2, S], F32, mix)
        kT = sb("kT", [P, 2, S], F32, mix)
        qmT = sb("qmT", [P, MHEADS, S], F32, mix)
        kmT = sb("kmT", [P, MHEADS, S], F32, mix)
        vm = sb("vm", [P, T, MEM_W], F32, mix)
        win_a = sb("win_a", [P, 4, PAD + S], F32, mix)
        pT = sb("pT", [P, 2, 512], F32, mix)
        w_pool_sb = sb("w_pool_sb", [P, 4, P], F32, mix)
        keys_rows = sb("keys_rows", [P, 2, KEYS], F32, mix)
        mask = sb("mask", [P, 2, P], F32, mix)
        scale_sb = sb("scale_sb", [P, 4], F32, mix)
        sinks = sb("sinks", [P, HEADS], F32, mix)
        pos_i = sb("pos_i", [P, T], I32, mix)
        pos_f = sb("pos_f", [P, T], F32, mix)
        ang = sb("ang", [P, 2, T, HALF], F32, mix)
        turns = sb("turns", [P, 2, T, HALF], F32, mix)
        cossin = sb("cossin", [P, 2, T, HALF], F32, mix)
        rt = sb("rt", [P, 4, HEADS * HALF], F32, mix)
        inv_count = sb("inv_count", [P, PAD], F32, mix)
        edge = sb("edge", [P, PAD], F32, mix)
        row_max = sb("row_max", [P, HEADS], F32, mix)
        neg_max = sb("neg_max", [P, HEADS], F32, mix)
        sink_in = sb("sink_in", [P, HEADS], F32, mix)
        sink_e = sb("sink_e", [P, HEADS], F32, mix)
        row_sum = sb("row_sum", [P, HEADS], F32, mix)
        row_inv = sb("row_inv", [P, HEADS], F32, mix)
        probs_flat = probs[:].rearrange("p h s -> p (h s)")
        q_rows = probs_flat[:, 0:T * SWA_W].rearrange("p (t c) -> p t c", t=T)
        span = 4 * (PAD + S)
        sums = [probs_flat[:, i * span:(i + 1) * span].rearrange("p (g s) -> p g s", g=4) for i in range(2)]
        means = probs_flat[:, 2 * span:2 * span + 4 * S].rearrange("p (g s) -> p g s", g=4)
        by_bank = lambda v: v[:].rearrange("p (b h) s -> p b (h s)", h=2)
        kmT_banks, qmT_banks, peer_qT = by_bank(kmT), by_bank(qmT), by_bank(scores_sb)
        mix.close()

        peer = ExitStack()
        experts = sb("experts", [P, T, PICKS], I32, peer)
        tails = sb("tails", [P, T, PICKS], I32, peer)
        chosen = sb("chosen", [P, T, 2, PHEADS, TOPK], F32, peer)
        window = sb("window", [P, 2, TOPK], I32, peer)
        tail_window = sb("tail_window", [P, 2, VRING], I32, peer)
        gate = sb("gate", [P, T, PHEADS, TOPK], F32, peer)
        gate_sum = sb("gate_sum", [P, PHEADS], F32, peer)
        hid = sb("hid", [P, T, PICKS], F32, peer)
        weight = sb("weight", [P, T, PICKS], F32, peer)
        part_u = ExitStack()
        pairT = sb("pairT", [P, T, 3, P], F32, part_u)
        key_hot = sb("key_hot", [P, ONES, KEYS], F32, part_u)
        weight_hot = sb("weight_hot", [P, ONES, KEYS], F32, part_u)
        rows = [sb(f"rows{i}", [P, D], F32, part_u) for i in range(RING)]
        part_u.close()
        v_lo_sb = sb("v_lo_sb", [P, VSPLIT, CH], F32R, peer)
        a_lo_sb = sb("a_lo_sb", [P, 2, S], F32R, peer)
        a_hi_sb = sb("a_hi_sb", [P, 2, S], F32R, peer)
        v_hi_sb = sb("v_hi_sb", [P, VSPLIT, CH], F32R, peer)
        v_raw = sb("v_raw", [P, VRAW, DENSE], F32, peer)
        tail_rows = [sb(f"tail_rows{i}", [P, TAIL], F32, peer) for i in range(VRING)]
        part_r = ExitStack()
        s12 = sb("s12", [P, T, 2 * PHEADS, KEYS], F32, part_r)
        left = sb("left", [P, 4 * KEYS], F32, part_r)
        cand = sb("cand", [P, STEP_H, TOPK, TOPK], F32, part_r)
        hit = sb("hit", [P, STEP_H, TOPK, TOPK], F32, part_r)
        top_v = sb("top_v", [P, 2 * STEP_H, TOPK], F32, part_r)
        top_i = sb("top_i", [P, 2 * STEP_H, TOPK], U32, part_r)
        top_if = sb("top_if", [P, 2 * STEP_H, TOPK], F32, part_r)
        best_v = sb("best_v", [P, STEP_H, TOPK], F32, part_r)
        best_p = sb("best_p", [P, STEP_H, TOPK], U32, part_r)
        digits = sb("digits", [P, 2, STEP_H, TOPK], U32, part_r)
        digits_f = sb("digits_f", [P, 2, STEP_H, TOPK], F32, part_r)
        part_r.close()
        part_a = ExitStack()
        spread = sb("spread", [P, KEYS, S], F32, part_a)
        part_a.close()
        gain2 = sb("gain2", [P, 2, D], F32, peer)
        peer.close()

        x_in, mem_in, small_in, gain_in, gain2_in, out_done = (
            sem(n) for n in ("x_in", "mem_in", "small_in", "gain_in", "gain2_in", "out_done"))
        w_in_sem = [sem(f"w_in{i}") for i in range(RAW)]
        consts = sem("consts")
        turned = sem("turned")
        turned_hi = sem("turned_hi")
        turned_lo = sem("turned_lo")
        w_hi, w_lo, w_used = sem("w_hi"), sem("w_lo"), sem("w_used")
        evac = sem("evac")
        qk_turned, qk_out = sem("qk_turned"), sem("qk_out")
        dve_step = sem("dve_step")
        roped = sem("roped")
        sc_done, sc_read = sem("sc_done"), sem("sc_read")
        msc_done = sem("msc_done")
        max_ready, exp_done, probs_ready = sem("max_ready"), sem("exp_done"), sem("probs_ready")
        pt_done, pt_out, pv_done = sem("pt_done"), sem("pt_out"), sem("pv_done")
        heads_hi, heads_lo = sem("heads_hi"), sem("heads_lo")
        keys_turned, keys_out = sem("keys_turned"), sem("keys_out")
        pooled, pool_done = sem("pooled"), sem("pool_done")
        var_ready, std_ready, normed = sem("var_ready"), sem("std_ready"), sem("normed")
        s12_done, s12_out = sem("s12_done"), sem("s12_out")
        routed, gate_in, gate_e = sem("routed"), sem("gate_in"), sem("gate_e")
        window_set = sem("window_set")
        row_in = [sem(f"row_in{i}") for i in range(RING)]
        rows_used = sem("rows_used")
        gelu_done, weighted = sem("gelu_done"), sem("weighted")
        pair_turned, pair_out = sem("pair_turned"), sem("pair_out")
        hot_key, hot_weight = sem("hot_key"), sem("hot_weight")
        built = sem("built")
        spread_out = sem("spread_out")
        v_in = [sem(f"v_in{i}") for i in range(VRAW)]
        v_hi = sem("v_hi")
        v_lo = sem("v_lo")
        v_used = sem("v_used")
        tail_in = [sem(f"tail_in{i}") for i in range(VRING)]
        tails_used = sem("tails_used")
        tail_set = sem("tail_set")
        turns_ready, sines = sem("turns_ready"), sem("sines")

        n_evac = [0]
        for _, kinds in GROUPS:
            n_evac.append(n_evac[-1] + 2 * len(kinds))

        def unit_of(g, j):
            return UNITS * g + j

        block = ctx.enter_context(nc.Block())

        @block.sync
        def _(sp):
            sp.dma_start(resid[:], x[0].rearrange("(t p) d -> p t d", p=P)).then_inc(x_in, 16)
            sp.dma_start(scores_sb[:].rearrange("p h s -> p (h s)").rearrange("p (t d) -> p t d", t=T),
                         mem[0].rearrange("(t p) d -> p t d", p=P)).then_inc(mem_in, 16)

            def source(g, j):
                r0, r1 = j * PAIR * P, (j + 1) * PAIR * P
                name = GROUPS[g][0]

                def piece(w, c0, c1):
                    return w[0, r0:r1, c0:c1].rearrange("(a p) n -> p a n", p=P)
                if name == "q":
                    return [(0, piece(w_in, POOL_W, POOL_W + SWA_W))]
                if name == "kv":
                    return [(0, piece(w_in, POOL_W + SWA_W, POOL_W + SWA_W + 2 * KV_W))]
                if name == "mem":
                    return [(0, piece(w_mem_kv, 0, 2 * MEM_W))]
                if name == "pool_qm":
                    q0 = POOL_W + SWA_W + 2 * KV_W
                    return [(0, piece(w_in, 0, POOL_W)), (POOL_W, piece(w_in, q0, q0 + MEM_W))]
                w = w_out if name.startswith("out") else w_peer_q
                c0 = COLS * int(name[-1])
                return [(0, piece(w, c0, c0 + COLS))]

            counts = [0] * RAW
            for g in range(len(GROUPS)):
                for j in range(UNITS):
                    u = unit_of(g, j)
                    if u >= RAW:
                        sp.wait_ge(w_lo, u - RAW + 1)
                    for c0, src in source(g, j):
                        sp.dma_start(raw[:, u % RAW, :, c0:c0 + src.shape[2]], src).then_inc(w_in_sem[u % RAW], 16)
                if g == OUT0:
                    sp.wait_ge(pt_done, 16)
                    sp.dma_start(probs_flat[:, 0:D], ln1_g[0:1, :].to_broadcast([P, D])).then_inc(gain_in, 16)
                    sp.dma_start(probs_flat[:, D:2 * D], ln1_b[0:1, :].to_broadcast([P, D])).then_inc(gain_in, 16)
            sp.wait_ge(rows_used, PRESET + T * PICKS)
            for part, (b0, b1) in enumerate(((0, 24), (24, BLOCKS // VRAW))):
                with sp.Fori(b0, b1) as i:
                    for k in range(VRAW):
                        sp.wait_ge(v_lo, i * (VRAW * DCH) + DCH * (k + 1))
                        sp.dma_start(v_raw[:, k, :], expert_v[0, bass.ds(i * (VRAW * P) + k * P, P), 0:DENSE]
                                     ).then_inc(v_in[k], 16)
                if part == 0:
                    sp.dma_start(gain2[:, 0, :], ln2_g[0:1, :].to_broadcast([P, D])).then_inc(gain2_in, 16)
                    sp.dma_start(gain2[:, 1, :], ln2_b[0:1, :].to_broadcast([P, D])).then_inc(gain2_in, 16)
            for t in range(T):
                sp.wait_ge(normed, T + t + 1)
                sp.dma_start(out[0, t * P:(t + 1) * P, :], resid[:, t, :]).then_inc(out_done, 16)
            sp.wait_ge(out_done, 16 * T)

        def pieces(g):
            return 2 if GROUPS[g][0] == "pool_qm" else 1

        def landed(u):
            n = 0
            for v in range(u % RAW, u + 1, RAW):
                n += 16 * pieces(v // UNITS)
            return n

        def width(g):
            return 512 * len(GROUPS[g][1])

        def q_heads(b):
            return ps[:, b, :].rearrange("p (m r c) -> p r m c", m=2, r=4)

        def q_pairs(b):
            return q_rows[:, b % 2, (b // 2) * 512:(b // 2 + 1) * 512].rearrange("p (r m c) -> p r m c", m=2, r=4)

        @block.gpsimd
        def _(pool):
            nc.gpsimd.memset(ident[:], 0.0).then_inc(consts, 1)
            nc.gpsimd.memset(mask[:], 0.0).then_inc(consts, 1)
            nc.gpsimd.memset(win_a[:], 0.0).then_inc(consts, 1)
            pool.wait_ge(consts, 3)
            nc.gpsimd.affine_select(out=ident[:], in_=ident[:], compare_op=ALU.not_equal, fill=1.0, base=0,
                                    pattern=[[-1, P]], channel_multiplier=1).then_inc(consts, 1)
            nc.gpsimd.affine_select(out=mask[:, 0, :], in_=mask[:, 0, :], compare_op=ALU.is_gt, fill=NEG, base=0,
                                    pattern=[[1, P]], channel_multiplier=-1).then_inc(consts, 1)
            nc.gpsimd.affine_select(out=mask[:, 1, :], in_=mask[:, 1, :], compare_op=ALU.is_ge, fill=NEG, base=0,
                                    pattern=[[-1, P]], channel_multiplier=1).then_inc(consts, 1)
            nc.gpsimd.iota(iota[:], [[1, KEYS]], base=0, channel_multiplier=0,
                           allow_small_or_imprecise_dtypes=True).then_inc(consts, 1)
            nc.gpsimd.iota(inv_count[:], [[1, PAD]], base=1, channel_multiplier=0,
                           allow_small_or_imprecise_dtypes=True).then_inc(consts, 1)

            for t in range(T):
                first = t * PICKS
                with pool.Fori(0, PHEADS // 2) as i:
                    pool.wait_ge(routed, i + (STEPS * t + 1))
                    for half in range(2):
                        pool.wait_ge(rows_used, i * (2 * TOPK) + (first + half * TOPK + RING))
                        nc.gpsimd.tensor_copy(window[:, half, :],
                                              experts[:, t, bass.ds(i * (2 * TOPK) + half * TOPK, TOPK)]
                                              ).then_inc(window_set, 1)
                        pool.wait_ge(window_set, i * 2 + (t * PHEADS + half + 1))
                        for k in range(TOPK):
                            pool.wait_ge(rows_used, i * (2 * TOPK) + (first + half * TOPK + k + 1 + TOPK))
                            pool.nop(nofuse=True)
                            nc.gpsimd.indirect_dma_start(
                                rows[k % RING][:], None, expert_u[0],
                                bass.IndirectOffsetOnAxis(ap=window[:, half, k:k + 1], axis=0)
                            ).then_inc(row_in[k % RING], 16)
            tail_table = expert_v[0].rearrange("e (c n) -> (e c) n", n=TAIL)
            pool.wait_ge(routed, STEPS * T + T)
            pool.wait_ge(rows_used, PRESET + T * PICKS)
            for t in range(T):
                with pool.Fori(0, PICKS // (2 * VRING)) as i:
                    for half in range(2):
                        n0 = t * PICKS + half * VRING
                        pool.wait_ge(tails_used, i * (2 * VRING) + (n0 + VRING))
                        nc.gpsimd.tensor_copy(tail_window[:, half, :],
                                              tails[:, t, bass.ds(i * (2 * VRING) + half * VRING, VRING)]
                                              ).then_inc(tail_set, 1)
                        pool.wait_ge(tail_set, i * 2 + (2 * t * (PICKS // (2 * VRING)) + half + 1))
                        for k in range(VRING):
                            pool.wait_ge(tails_used, i * (2 * VRING) + (n0 + k + 1 + VRING))
                            pool.nop(nofuse=True)
                            nc.gpsimd.indirect_dma_start(
                                tail_rows[k][:], None, tail_table,
                                bass.IndirectOffsetOnAxis(ap=tail_window[:, half, k:k + 1], axis=0)
                            ).then_inc(tail_in[k], 16)

        @block.scalar
        def _(act):
            act.dma_start(pos_i[:], positions[0].rearrange("(t p) -> p t", p=P),
                          allow_slow_non_contiguous=True).then_inc(small_in, 16)
            act.dma_start(scale_sb[:], pool_scale[0].rearrange("(c p) -> p c", p=P),
                          allow_slow_non_contiguous=True).then_inc(small_in, 16)
            act.dma_start(sinks[:], attn_sinks[0:1, :].to_broadcast([P, HEADS])).then_inc(small_in, 16)
            act.dma_start(w_pool_sb[:], w_pool[0].rearrange("g c d -> c g d")).then_inc(small_in, 16)
            act.dma_start(keys_rows[:, 0, :], sub_keys_1[0]).then_inc(small_in, 16)
            act.dma_start(keys_rows[:, 1, :], sub_keys_2[0]).then_inc(small_in, 16)

            def turn_out(first, dst):
                for b in range(KC // 2):
                    act.wait_ge(turned, first + b + 1)
                    nc.scalar.activation(dst[:, 2 * b:2 * b + 2, :].rearrange("p a s -> p (a s)"),
                                         ps[:, 4 + (first + b) % 4, :], ACT.Copy).then_inc(turned_hi, 1)

            def split(g):
                for j in range(UNITS):
                    u = unit_of(g, j)
                    act.wait_ge(w_in_sem[u % RAW], landed(u))
                    if u >= SPLIT:
                        act.wait_ge(w_used, u - SPLIT + 1)
                    nc.scalar.activation(w_hi_sb[:, u % SPLIT, :, 0:width(g)], raw[:, u % RAW, :, 0:width(g)],
                                         ACT.Copy).then_inc(w_hi, 1)

            def read_out(g, banks, dst):
                act.wait_ge(w_used, unit_of(g, UNITS))
                for b in banks:
                    nc.scalar.activation(dst(b), ps[:, b, :], ACT.Copy).then_inc(evac, 1)

            turn_out(0, xT_hi)
            turn_out(8, yT_hi)
            act.wait_ge(turns_ready, 1)
            nc.scalar.activation(cossin[:], ang[:], ACT.Sin).then_inc(sines, 1)

            split(Q)
            for b in (0, 2):
                act.wait_ge(w_used, unit_of(Q, UNITS))
                nc.scalar.activation(q_pairs(b), q_heads(b), ACT.Copy).then_inc(evac, 1)
            split(KV)
            read_out(KV, (0,), lambda b: kv[:, b, :])
            split(MEM)
            read_out(MEM, (0, 2), lambda b: kmT_banks[:, b, :] if b < 2 else vm[:, b - 2, :])
            for i in range(5):
                act.wait_ge(qk_turned, i + 1)
                dst = qT[:, 2 * i:2 * i + 2, :] if i < 4 else kT[:]
                nc.scalar.activation(dst.rearrange("p a s -> p (a s)"), ps[:, 4 + i % 4, :], ACT.Copy
                                     ).then_inc(qk_out, 1)
            split(POOLQM)
            read_out(POOLQM, (2,), lambda b: qmT_banks[:, b - 2, :])

            act.wait_ge(pool_done, 1)
            for g in range(4):
                nc.scalar.activation(yT_hi[:, g, :], ps[:, g // 2, (g % 2) * S:(g % 2 + 1) * S], ACT.Copy,
                                     scale=scale_sb[:, g:g + 1]).then_inc(heads_hi, 1)

            def pt_copy(f):
                act.wait_ge(pt_done, f + 1)
                if f >= 2:
                    act.wait_ge(pv_done, f - 1)
                nc.scalar.activation(pT[:, f % 2, :], ps[:, 4 + f % 2, :], ACT.Copy).then_inc(pt_out, 1)

            f = 0
            for t in range(T):
                nk = P * (t + 1)
                act.wait_ge(max_ready, t + 1)
                for h in range(HEADS):
                    last = nc.scalar.activation(probs[:, h, 0:nk], scores_sb[:, h, 0:nk], ACT.Exp,
                                                bias=neg_max[:, h:h + 1], accum_out=row_sum[:, h:h + 1])
                last = nc.scalar.activation(sink_e[:], sink_in[:], ACT.Exp)
                last.then_inc(exp_done, 1)
                for _ in range(4 * (t + 1)):
                    pt_copy(f)
                    f += 1
                act.wait_ge(pv_done, f)
                for b in range(2):
                    nc.scalar.activation(yT_hi[:, 4 + 4 * b:8 + 4 * b, t * P:(t + 1) * P],
                                         ps[:, 6 + b, :].rearrange("p (c s) -> p c s", c=4), ACT.Copy
                                         ).then_inc(heads_hi, 1)
            act.wait_ge(max_ready, T + 1)
            for n in range(T * MHEADS):
                last = nc.scalar.activation(probs[:, n, :], ps[:, n // 2, (n % 2) * S:(n % 2 + 1) * S], ACT.Exp,
                                            bias=neg_max[:, n:n + 1], scale=float(MHD) ** -0.5,
                                            accum_out=row_sum[:, n:n + 1])
            last.then_inc(exp_done, 1)
            for _ in range(4):
                pt_copy(f)
                f += 1
            act.wait_ge(pv_done, f)
            for t in range(T):
                nc.scalar.activation(yT_hi[:, 12:16, t * P:(t + 1) * P],
                                     ps[:, 6 + t, :].rearrange("p (c s) -> p c s", c=4), ACT.Copy
                                     ).then_inc(heads_hi, 1)
            split(OUT0)
            split(OUT1)
            for t in range(T):
                act.wait_ge(var_ready, t + 1)
                nc.scalar.activation(rstd[:, t, 0:1], rstd[:, t, 1:2], ACT.Sqrt).then_inc(std_ready, 1)
            turn_out(16, xT_hi)
            split(PEER0)
            read_out(PEER0, (0, 2), lambda b: peer_qT[:, b, :])
            split(PEER1)
            read_out(PEER1, (0, 2), lambda b: peer_qT[:, 4 + b, :])

            act.wait_ge(keys_turned, 1)
            nc.scalar.activation(keysT[:].rearrange("p a k -> p (a k)"), ps[:, 4, 0:2 * KEYS], ACT.Copy
                                 ).then_inc(keys_out, 1)

            act.sem_inc(spread_out, 4)
            for t in range(T):
                for b in range(4):
                    act.wait_ge(s12_done, 4 * t + b + 1)
                    nc.scalar.activation(s12[:, t, 4 * b:4 * b + 4, :].rearrange("p a s -> p (a s)"),
                                         ps[:, 4 * (1 - t) + b, :], ACT.Copy).then_inc(s12_out, 1)
            for t in range(T):
                act.wait_ge(gate_in, STEPS * (t + 1))
                nc.scalar.activation(gate[:, t], gate[:, t], ACT.Exp).then_inc(gate_e, 1)

            for t in range(T):
                act.wait_ge(rows_used, PRESET + (t + 1) * PICKS)
                nc.scalar.activation(weight[:, t, :], hid[:, t, :], ACT.Gelu).then_inc(gelu_done, 1)
                act.wait_ge(pair_turned, t + 1)
                nc.scalar.activation(pairT[:, t].rearrange("p a s -> p (a s)"), ps[:, t, 0:3 * P], ACT.Copy
                                     ).then_inc(pair_out, 1)
                with act.Fori(0, P // 16) as i:
                    for q in range(4):
                        act.wait_ge(built, i * 16 + (ONES + P * t + 4 * q + 4))
                        act.nop(nofuse=True)
                        nc.scalar.activation(
                            spread[:, :, bass.ds(i * 16 + (P * t + 4 * q), 4)].rearrange("p k s -> p s k"),
                            ps[:, 4 + q, :].rearrange("p (s k) -> p s k", s=4), ACT.Copy).then_inc(spread_out, 1)

            act.wait_ge(spread_out, 4 + S // 4)
            with act.Fori(0, BLOCKS // VRAW) as i:
                for k in range(VRAW):
                    act.wait_ge(v_used, i * (VRAW * DCH) + (DCH * k + 1))
                    act.nop(nofuse=True)
                    nc.scalar.activation(a_hi_sb[:, k % 2, :], spread[:, bass.ds(i * VRAW + k, 1), :].rearrange(
                        "p a s -> p (a s)"), ACT.Copy).then_inc(v_hi, 1)
                    act.wait_ge(v_in[k], i * 16 + 16)
                    for c in range(DCH):
                        act.wait_ge(v_used, i * (VRAW * DCH) + (DCH * k + c + 1))
                        nc.scalar.activation(v_hi_sb[:, (DCH * k + c) % VSPLIT, :],
                                             v_raw[:, k, c * CH:(c + 1) * CH], ACT.Copy).then_inc(v_hi, 1)
            for t in range(T):
                act.wait_ge(var_ready, T + t + 1)
                nc.scalar.activation(rstd[:, t, 0:1], rstd[:, t, 1:2], ACT.Sqrt).then_inc(std_ready, 1)

        @block.vector
        def _(dve):
            steps = [0]

            def link(ins):
                steps[0] += 1
                ins.then_inc(dve_step, 1)
                dve.wait_ge(dve_step, steps[0])

            def turn_low(first, hi, lo):
                for b in range(KC // 2):
                    dve.wait_ge(turned_hi, first + b + 1)
                    nc.vector.tensor_tensor(lo[:, 2 * b:2 * b + 2, :].rearrange("p a s -> p (a s)"),
                                            ps[:, 4 + (first + b) % 4, :],
                                            hi[:, 2 * b:2 * b + 2, :].rearrange("p a s -> p (a s)").bitcast(F32),
                                            ALU.subtract).then_inc(turned_lo, 1)

            def split(g):
                for j in range(UNITS):
                    u = unit_of(g, j)
                    dve.wait_ge(w_hi, u + 1)
                    nc.vector.tensor_tensor(w_lo_sb[:, u % SPLIT, :, 0:width(g)], raw[:, u % RAW, :, 0:width(g)],
                                            w_hi_sb[:, u % SPLIT, :, 0:width(g)].bitcast(F32),
                                            ALU.subtract).then_inc(w_lo, 1)

            def read_out(g, banks, dst):
                dve.wait_ge(w_used, unit_of(g, UNITS))
                for b in banks:
                    nc.vector.tensor_copy(dst(b), ps[:, b, :]).then_inc(evac, 1)

            dve.wait_ge(small_in, 16 * 6)
            link(nc.vector.tensor_copy(pos_f[:], pos_i[:]))
            for j in range(HALF):
                last = nc.vector.tensor_scalar(ang[:, 1, :, j], pos_f[:], float(THETA ** (-2.0 * j / ROPE)), None,
                                               ALU.mult)
            link(last)
            link(nc.vector.tensor_scalar(ang[:, 0], ang[:, 1], PI / 2, None, ALU.add))
            link(nc.vector.tensor_scalar(turns[:], ang[:], 0.5 / PI, ROUND, ALU.mult, ALU.add))
            link(nc.vector.tensor_scalar(turns[:], turns[:], ROUND, None, ALU.subtract))
            for part in TWO_PI:
                link(nc.vector.scalar_tensor_tensor(out=ang[:], in0=turns[:], scalar=-part, in1=ang[:],
                                                    op0=ALU.mult, op1=ALU.add))
            nc.vector.tensor_scalar(ang[:], ang[:], -3.1415925, 3.1415925, ALU.max, ALU.min
                                    ).then_inc(turns_ready, 1)
            dve.wait_ge(consts, 8)
            link(nc.vector.reciprocal(inv_count[:], inv_count[:]))

            turn_low(0, xT_hi, xT_lo)
            turn_low(8, yT_hi, yT_lo)
            split(Q)
            for b in (1, 3):
                dve.wait_ge(w_used, unit_of(Q, UNITS))
                nc.vector.tensor_copy(q_pairs(b), q_heads(b)).then_inc(evac, 1)
            split(KV)
            read_out(KV, (1,), lambda b: kv[:, b, :])
            dve.wait_ge(sines, 1)
            dve.wait_ge(evac, n_evac[KV + 1])
            turned_rows = 0
            for t in range(T):
                for rows_, n in ((q_rows[:, t, :], HEADS), (kv[:, t, 0:KV_W], KV_W // HD)):
                    heads = rows_.rearrange("p (h c) -> p h c", c=HD)
                    a, b = heads[:, :, 0:HALF], heads[:, :, HALF:ROPE]
                    cos = cossin[:, 0, t, :].unsqueeze(1).to_broadcast([P, n, HALF])
                    sin = cossin[:, 1, t, :].unsqueeze(1).to_broadcast([P, n, HALF])
                    r = [rt[:, k, 0:n * HALF].rearrange("p (h c) -> p h c", c=HALF) for k in range(4)]
                    nc.vector.tensor_tensor(r[0], a, cos, ALU.mult)
                    nc.vector.tensor_tensor(r[1], b, sin, ALU.mult)
                    nc.vector.tensor_tensor(r[2], b, cos, ALU.mult)
                    link(nc.vector.tensor_tensor(r[3], a, sin, ALU.mult))
                    nc.vector.tensor_tensor(a, r[0], r[1], ALU.subtract)
                    nc.vector.tensor_tensor(b, r[2], r[3], ALU.add).then_inc(roped, 1)
                    turned_rows += 1
                    dve.wait_ge(roped, turned_rows)
            split(MEM)
            read_out(MEM, (1, 3), lambda b: kmT_banks[:, b, :] if b < 2 else vm[:, b - 2, :])
            split(POOLQM)
            read_out(POOLQM, (3,), lambda b: qmT_banks[:, b - 2, :])
            for b in (0, 1):
                last = nc.vector.tensor_copy(win_a[:, 2 * b:2 * b + 2, PAD:],
                                             ps[:, b, :].rearrange("p (g s) -> p g s", g=2))
                last.then_inc(evac, 1)

            dve.wait_ge(evac, n_evac[POOLQM + 1])
            dve.wait_ge(qk_turned, 4)
            for dst in sums:
                last = nc.vector.memset(dst[:, :, 0:PAD], 0.0)
            link(last)
            src = win_a
            for lev in range(4):
                dst, back, w = sums[lev % 2], 1 << lev, WINDOWS[lev]
                nc.vector.tensor_scalar(edge[:, 0:w], inv_count[:, 0:w], float(w), None, ALU.mult)
                link(nc.vector.tensor_tensor(dst[:, lev:4, PAD:], src[:, lev:4, PAD:],
                                             src[:, lev:4, PAD - back:PAD + S - back], ALU.add))
                link(nc.vector.tensor_tensor(dst[:, lev, PAD:PAD + w], dst[:, lev, PAD:PAD + w], edge[:, 0:w],
                                             ALU.mult))
                nc.vector.scalar_tensor_tensor(out=means[:, lev, :], in0=dst[:, lev, PAD:], scalar=1.0 / w,
                                               in1=win_a[:, lev, PAD:], op0=ALU.mult, op1=ALU.subtract
                                               ).then_inc(pooled, 1)
                dve.wait_ge(pooled, lev + 1)
                src = dst
            for g in range(4):
                dve.wait_ge(heads_hi, 2 * (g // 2) + 2)
                nc.vector.scalar_tensor_tensor(out=yT_lo[:, g, :], in0=ps[:, g // 2, (g % 2) * S:(g % 2 + 1) * S],
                                               scalar=scale_sb[:, g:g + 1], in1=yT_hi[:, g, :].bitcast(F32),
                                               op0=ALU.mult, op1=ALU.subtract).then_inc(heads_lo, 1)

            for t in range(T):
                nk = P * (t + 1)
                for p in range(4):
                    dve.wait_ge(sc_done, 4 * t + p + 1)
                    if t and p == 0:
                        dve.wait_ge(exp_done, t)
                    for m in range(2):
                        h0 = 8 * (p // 2) + 4 * m + 2 * (p % 2)
                        sc = ps[:, 2 * (p % 2) + m, 0:2 * nk].rearrange("p (h s) -> p h s", h=2)
                        mk = mask[:, 1 - t:2, :].rearrange("p a s -> p (a s)").unsqueeze(1).to_broadcast([P, 2, nk])
                        last = nc.vector.scalar_tensor_tensor(out=scores_sb[:, h0:h0 + 2, 0:nk], in0=sc,
                                                              scalar=float(HD) ** -0.5, in1=mk,
                                                              op0=ALU.mult, op1=ALU.add)
                        last.then_inc(sc_read, 1)
                dve.wait_ge(sc_read, 8 * (t + 1))
                link(nc.vector.reduce_max(row_max[:], scores_sb[:, :, 0:nk], AX.X))
                link(nc.vector.tensor_tensor(row_max[:], row_max[:], sinks[:], ALU.max))
                nc.vector.tensor_scalar(neg_max[:], row_max[:], -1.0, None, ALU.mult)
                nc.vector.tensor_tensor(sink_in[:], sinks[:], row_max[:], ALU.subtract).then_inc(max_ready, 1)
                dve.wait_ge(exp_done, t + 1)
                link(nc.vector.tensor_tensor(row_sum[:], row_sum[:], sink_e[:], ALU.add))
                link(nc.vector.reciprocal(row_inv[:], row_sum[:]))
                nc.vector.tensor_tensor(probs[:, :, 0:nk], probs[:, :, 0:nk],
                                        row_inv[:].unsqueeze(2).to_broadcast([P, HEADS, nk]), ALU.mult
                                        ).then_inc(probs_ready, 1)
                for b in range(2):
                    dve.wait_ge(heads_hi, 4 + 2 * t + b + 1)
                    nc.vector.tensor_tensor(yT_lo[:, 4 + 4 * b:8 + 4 * b, t * P:(t + 1) * P],
                                            ps[:, 6 + b, :].rearrange("p (c s) -> p c s", c=4),
                                            yT_hi[:, 4 + 4 * b:8 + 4 * b, t * P:(t + 1) * P].bitcast(F32),
                                            ALU.subtract).then_inc(heads_lo, 1)
            for b in range(4):
                dve.wait_ge(msc_done, b + 1)
                last = nc.vector.reduce_max(row_max[:, 2 * b:2 * b + 2],
                                            ps[:, b, :].rearrange("p (h s) -> p h s", h=2), AX.X)
            link(last)
            nc.vector.tensor_scalar(neg_max[:, 0:8], row_max[:, 0:8], -float(MHD) ** -0.5, None, ALU.mult
                                    ).then_inc(max_ready, 1)
            dve.wait_ge(exp_done, T + 1)
            link(nc.vector.reciprocal(row_inv[:, 0:8], row_sum[:, 0:8]))
            nc.vector.tensor_tensor(probs[:, 0:8, :], probs[:, 0:8, :],
                                    row_inv[:, 0:8].unsqueeze(2).to_broadcast([P, 8, S]), ALU.mult
                                    ).then_inc(probs_ready, 1)
            for t in range(T):
                dve.wait_ge(heads_hi, 4 + 2 * T + t + 1)
                nc.vector.tensor_tensor(yT_lo[:, 12:16, t * P:(t + 1) * P],
                                        ps[:, 6 + t, :].rearrange("p (c s) -> p c s", c=4),
                                        yT_hi[:, 12:16, t * P:(t + 1) * P].bitcast(F32),
                                        ALU.subtract).then_inc(heads_lo, 1)

            for g in (OUT0, OUT1):
                split(g)
                dve.wait_ge(w_used, unit_of(g, UNITS))
                for b in range(4):
                    c0 = COLS * (g - OUT0) + 512 * (b // 2)
                    cols = resid[:, b % 2, c0:c0 + 512]
                    nc.vector.scalar_tensor_tensor(out=cols, in0=cols, scalar=ALPHA, in1=ps[:, b, :],
                                                   op0=ALU.mult, op1=ALU.add).then_inc(evac, 1)

            def norm(tile, t, n, gain, shift):
                for c in range(4):
                    last = nc.vector.bn_stats(stats[:, t, c, :], tile[:, 512 * c:512 * (c + 1)])
                link(last)
                link(nc.vector.bn_aggr(moments[:, t, :], stats[:, t].rearrange("p c k -> p (c k)")))
                nc.vector.tensor_scalar(rstd[:, t, 1:2], moments[:, t, 1:2], EPS, None, ALU.add
                                        ).then_inc(var_ready, 1)
                dve.wait_ge(std_ready, n + 1)
                link(nc.vector.reciprocal(rstd[:, t, 2:3], rstd[:, t, 0:1]))
                link(nc.vector.tensor_tensor(rstd[:, t, 3:4], rstd[:, t, 2:3], rstd[:, t, 2:3], ALU.mult))
                link(nc.vector.tensor_tensor(rstd[:, t, 3:4], rstd[:, t, 3:4], rstd[:, t, 1:2], ALU.mult))
                link(nc.vector.tensor_scalar(rstd[:, t, 3:4], rstd[:, t, 3:4], -0.5, 1.5, ALU.mult, ALU.add))
                link(nc.vector.tensor_tensor(rstd[:, t, 2:3], rstd[:, t, 2:3], rstd[:, t, 3:4], ALU.mult))
                link(nc.vector.tensor_scalar(tile, tile, moments[:, t, 0:1], rstd[:, t, 2:3],
                                             ALU.subtract, ALU.mult))
                link(nc.vector.tensor_tensor(tile, tile, gain, ALU.mult))
                nc.vector.tensor_tensor(tile, tile, shift, ALU.add).then_inc(normed, 1)

            dve.wait_ge(evac, n_evac[OUT1 + 1])
            dve.wait_ge(gain_in, 32)
            for t in range(T):
                norm(resid[:, t, :], t, t, probs_flat[:, 0:D], probs_flat[:, D:2 * D])
            turn_low(16, xT_hi, xT_lo)
            split(PEER0)
            read_out(PEER0, (1, 3), lambda b: peer_qT[:, b, :])
            split(PEER1)
            read_out(PEER1, (1, 3), lambda b: peer_qT[:, 4 + b, :])
            dve.sem_inc(rows_used, PRESET)
            dve.sem_inc(v_lo, VRAW * DCH)
            dve.sem_inc(tails_used, VPRESET)

            def top16(n, values, rest, best, index):
                for r in range(n):
                    last = nc.vector.max(best(r)[:, 0:8], values(r))
                link(last)
                for r in range(n):
                    last = nc.vector.match_replace(rest(r), best(r)[:, 0:8], values(r), LOWEST)
                link(last)
                for r in range(n):
                    last = nc.vector.max(best(r)[:, 8:16], rest(r))
                link(last)
                for r in range(n):
                    nc.vector.max_index(index(r)[:, 0:8], best(r)[:, 0:8], values(r))
                    last = nc.vector.max_index(index(r)[:, 8:16], best(r)[:, 8:16], rest(r))
                link(last)

            def route(t, step):
                n = STEPS * t + step
                heads = slice(STEP_H * step, STEP_H * (step + 1))
                dve.wait_ge(s12_out, n + 1)
                left3 = left[:].rearrange("p (r k) -> p r k", k=KEYS)
                top16(2 * STEP_H, lambda r: s12[:, t, 2 * STEP_H * step + r, :], lambda r: left3[:, r, :],
                      lambda r: top_v[:, r, :], lambda r: top_i[:, r, :])
                nc.vector.tensor_copy(top_if[:], top_i[:])
                tv = top_v[:].rearrange("p (h a) k -> p h a k", a=2)
                wide = [P, STEP_H, TOPK, TOPK]
                link(nc.vector.tensor_tensor(cand[:], tv[:, :, 0, :].unsqueeze(3).to_broadcast(wide),
                                             tv[:, :, 1, :].unsqueeze(2).to_broadcast(wide), ALU.add))
                left4 = left[:].rearrange("p (h k) -> p h k", k=TOPK * TOPK)
                top16(STEP_H, lambda h: cand[:, h].rearrange("p a b -> p (a b)"), lambda h: left4[:, h, :],
                      lambda h: best_v[:, h, :], lambda h: best_p[:, h, :])
                nc.vector.tensor_tensor(gate[:, t, heads], best_v[:],
                                        best_v[:, :, 0:1].to_broadcast([P, STEP_H, TOPK]),
                                        ALU.subtract).then_inc(gate_in, 1)

            def choose(t, step):
                heads = slice(STEP_H * step, STEP_H * (step + 1))
                wide = [P, STEP_H, TOPK, TOPK]
                nc.vector.tensor_scalar(digits[:, 0], best_p[:], 4, None, ALU.logical_shift_right)
                link(nc.vector.tensor_scalar(digits[:, 1], best_p[:], TOPK - 1, None, ALU.bitwise_and))
                link(nc.vector.tensor_copy(digits_f[:], digits[:]))
                tif = top_if[:].rearrange("p (h a) k -> p h a k", a=2)
                for a in range(2):
                    link(nc.vector.tensor_tensor(
                        hit[:], digits_f[:, a].unsqueeze(3).to_broadcast(wide),
                        iota[:, 0:TOPK].unsqueeze(1).unsqueeze(1).to_broadcast(wide), ALU.is_equal))
                    link(nc.vector.tensor_tensor(
                        hit[:], hit[:], tif[:, :, a, :].unsqueeze(2).to_broadcast(wide), ALU.mult))
                    link(nc.vector.reduce_sum(chosen[:, t, a, heads], hit[:], AX.X))
                picks = experts[:, t, :].rearrange("p (h k) -> p h k", h=PHEADS)[:, heads]
                nc.vector.scalar_tensor_tensor(out=picks, in0=chosen[:, t, 0, heads],
                                               scalar=float(KEYS), in1=chosen[:, t, 1, heads],
                                               op0=ALU.mult, op1=ALU.add).then_inc(routed, 1)

            def tails_of(t):
                first_key, second = (chosen[:, t, a].rearrange("p h k -> p (h k)") for a in range(2))
                link(nc.vector.scalar_tensor_tensor(out=left[:, t * PICKS:(t + 1) * PICKS], in0=first_key, scalar=float(KEYS),
                                                    in1=second, op0=ALU.mult, op1=ALU.add))
                nc.vector.tensor_scalar(tails[:, t, :], left[:, t * PICKS:(t + 1) * PICKS], float(D // TAIL), float(D // TAIL - 1),
                                        ALU.mult, ALU.add).then_inc(routed, 1)

            def gathered(i, first, k, turn):
                dve.wait_ge(row_in[k % RING], i * (16 * turn // RING) + 16 * ((first + k) // RING + 1))

            def hidden(t, k, col):
                nc.vector.scalar_tensor_tensor(
                    out=rows[k % RING][:], in0=rows[k % RING][:], scalar=1.0, in1=resid[:, t, :],
                    op0=ALU.mult, op1=ALU.mult, accum_out=hid[:, t, bass.ds(col, 1)]).then_inc(rows_used, 1)

            def weights(t):
                dve.wait_ge(gate_e, t + 1)
                link(nc.vector.reduce_sum(gate_sum[:], gate[:, t], AX.X))
                link(nc.vector.reciprocal(gate_sum[:], gate_sum[:]))
                link(nc.vector.tensor_tensor(gate[:, t], gate[:, t],
                                             gate_sum[:].unsqueeze(2).to_broadcast([P, PHEADS, TOPK]), ALU.mult))
                dve.wait_ge(gelu_done, t + 1)
                nc.vector.tensor_tensor(weight[:, t, :], weight[:, t, :], gate[:, t].rearrange("p h k -> p (h k)"),
                                        ALU.mult).then_inc(weighted, 1)

            def scatter_rows(i, t, k):
                if k % 8 == 0:
                    dve.wait_ge(built, i * TOPK + (t * P + k + 8))
                    nc.vector.tensor_tensor(
                        key_hot[:, k % ONES:k % ONES + 8, :], iota[:].unsqueeze(1).to_broadcast([P, 8, KEYS]),
                        pairT[:, t, 1, bass.ds(i * TOPK + k, 8)].unsqueeze(2).to_broadcast([P, 8, KEYS]),
                        ALU.is_equal).then_inc(hot_key, 1)
                nc.vector.tensor_scalar(weight_hot[:, k % ONES, :], iota[:],
                                        pairT[:, t, 0, bass.ds(i * TOPK + k, 1)],
                                        pairT[:, t, 2, bass.ds(i * TOPK + k, 1)],
                                        ALU.is_equal, ALU.mult).then_inc(hot_weight, 1)

            head_steps = [(t, step) for t in range(T) for step in range(STEPS)]
            route(0, 0)
            choose(0, 0)
            for n in range(2, 2 * PHEADS + 2):
                first = (n - 2) * (TOPK // 2)
                with dve.Fori(0, 2) as i:
                    for k in range(RING):
                        gathered(i, first, k, RING)
                        hidden(0, k, i * RING + (first + k))
                if n < 2 * PHEADS:
                    (route, choose)[n % 2](*head_steps[n // 2])
            for t in range(T):
                tails_of(t)
            weights(0)
            dve.wait_ge(pair_out, 1)
            with dve.Fori(0, PHEADS) as i:
                for k in range(TOPK):
                    gathered(i, PICKS, k, TOPK)
                    hidden(1, k, i * TOPK + k)
                    scatter_rows(i, 0, k)
            weights(1)
            dve.wait_ge(rows_used, PRESET + T * PICKS)
            link(nc.vector.tensor_scalar(resid[:, :, DENSE:], resid[:, :, DENSE:], ALPHA, None, ALU.mult))
            dve.wait_ge(pair_out, 2)
            with dve.Fori(0, PHEADS) as i:
                for k in range(TOPK):
                    scatter_rows(i, 1, k)
            dve.wait_ge(built, ONES + S)
            dve.wait_ge(spread_out, 4 + S // 4)
            half = BLOCKS // VRAW // T
            for t in range(T):
                with dve.Fori(0, half) as i:
                    for k in range(VRAW):
                        b = VRAW * half * t + k
                        dve.wait_ge(v_hi, i * (VRAW * (DCH + 1)) + ((DCH + 1) * b + 1))
                        nc.vector.tensor_tensor(a_lo_sb[:, k % 2, :], spread[:, bass.ds(i * VRAW + b, 1), :].rearrange(
                            "p a s -> p (a s)"), a_hi_sb[:, k % 2, :].bitcast(F32), ALU.subtract)
                        for c in range(DCH):
                            dve.wait_ge(v_hi, i * (VRAW * (DCH + 1)) + ((DCH + 1) * b + c + 2))
                            slot = (DCH * k + c) % VSPLIT
                            nc.vector.tensor_tensor(v_lo_sb[:, slot, :], v_raw[:, k, c * CH:(c + 1) * CH],
                                                    v_hi_sb[:, slot, :].bitcast(F32), ALU.subtract).then_inc(v_lo, 1)
                        for q in range(2 * k, 2 * k + 2):
                            n = t * PICKS + q
                            dve.wait_ge(tail_in[q % VRING], i * (2 * VRAW * 16 // VRING) + 16 * (n // VRING + 1))
                            dve.wait_ge(tails_used, i * (2 * VRAW) + (n + VPRESET))
                            nc.vector.scalar_tensor_tensor(
                                out=resid[:, t, DENSE:], in0=tail_rows[q % VRING][:],
                                scalar=weight[:, t, bass.ds(i * (2 * VRAW) + q, 1)], in1=resid[:, t, DENSE:],
                                op0=ALU.mult, op1=ALU.add).then_inc(tails_used, 1)
            dve.wait_ge(tails_used, VPRESET + T * PICKS)
            dve.wait_ge(v_used, VSPLIT + DCH * BLOCKS)
            dve.wait_ge(gain2_in, 32)
            for t in range(T):
                for c in range(DCH):
                    cols = resid[:, t, c * CH:(c + 1) * CH]
                    last = nc.vector.scalar_tensor_tensor(out=cols, in0=cols, scalar=ALPHA, in1=ps[:, DCH * t + c, :],
                                                          op0=ALU.mult, op1=ALU.add)
                link(last)
                norm(resid[:, t, :], t, T + t, gain2[:, 0, :], gain2[:, 1, :])

        @block.tensor
        def _(pe):
            def turn(first, src):
                for b in range(KC // 2):
                    if first + b >= 4:
                        pe.wait_ge(turned_lo, first + b - 3)
                    for c in range(2):
                        for t in range(T):
                            k = 2 * b + c
                            last = nc.tensor.transpose(ps[:, 4 + (first + b) % 4, (2 * c + t) * P:(2 * c + t + 1) * P],
                                                       src(t)[:, k * P:(k + 1) * P], ident[:])
                    last.then_inc(turned, 1)

            def group(g, hi, lo):
                if g:
                    pe.wait_ge(evac, n_evac[g])
                for j in range(UNITS):
                    u = unit_of(g, j)
                    pe.wait_ge(w_lo, u + 1)
                    for a in range(PAIR):
                        k = PAIR * j + a
                        first, final = k == 0, k == KC - 1
                        for half, kind in enumerate(GROUPS[g][1]):
                            wh = w_hi_sb[:, u % SPLIT, a, 512 * half:512 * half + 512]
                            wl = w_lo_sb[:, u % SPLIT, a, 512 * half:512 * half + 512]
                            if kind == "R":
                                for t in range(T):
                                    o = ps[:, 2 * half + t, :]
                                    xh, xl = (v[:, k, t * P:(t + 1) * P] for v in (hi, lo))
                                    nc.tensor.matmul(o, xh, wh, start=first, stop=False)
                                    nc.tensor.matmul(o, xh, wl, start=False, stop=False)
                                    last = nc.tensor.matmul(o, xl, wh, start=False, stop=final)
                            else:
                                for b in range(4):
                                    o = ps[:, 2 * half + b // 2, (b % 2) * S:(b % 2 + 1) * S]
                                    wbh, wbl = wh[:, b * P:(b + 1) * P], wl[:, b * P:(b + 1) * P]
                                    nc.tensor.matmul(o, wbh, hi[:, k, :], start=first and b % 2 == 0, stop=False,
                                                     skip_group_check=True)
                                    nc.tensor.matmul(o, wbh, lo[:, k, :], start=False, stop=False,
                                                     skip_group_check=True)
                                    last = nc.tensor.matmul(o, wbl, hi[:, k, :], start=False, stop=final,
                                                            skip_group_check=True)
                    last.then_inc(w_used, 1)

            pe.wait_ge(consts, 4)
            pe.wait_ge(x_in, 16)
            turn(0, lambda t: resid[:, t, :])
            pe.wait_ge(mem_in, 16)
            mem_rows = scores_sb[:].rearrange("p h s -> p (h s)")
            turn(8, lambda t: mem_rows[:, t * D:(t + 1) * D])
            pe.wait_ge(turned_lo, 16)
            group(Q, xT_hi, xT_lo)
            group(KV, xT_hi, xT_lo)
            group(MEM, yT_hi, yT_lo)
            pe.wait_ge(roped, 2 * T)
            for i in range(5):
                if i == 4:
                    pe.wait_ge(qk_out, 1)
                for c in range(2):
                    for t in range(T):
                        j = 2 * i + c
                        src = q_rows[:, t, j * P:(j + 1) * P] if i < 4 else kv[:, t, c * P:(c + 1) * P]
                        last = nc.tensor.transpose(ps[:, 4 + i % 4, (2 * c + t) * P:(2 * c + t + 1) * P], src, ident[:])
                last.then_inc(qk_turned, 1)
            group(POOLQM, xT_hi, xT_lo)
            pe.wait_ge(evac, n_evac[POOLQM + 1])
            pe.wait_ge(pooled, 4)
            for g in range(4):
                last = nc.tensor.matmul(ps[:, g // 2, (g % 2) * S:(g % 2 + 1) * S], w_pool_sb[:, g, :],
                                        means[:, g, :], start=True, stop=True)
            last.then_inc(pool_done, 1)
            pe.wait_ge(heads_lo, 4)
            pe.wait_ge(qk_out, 5)

            f = 0
            for t in range(T):
                nk = P * (t + 1)
                for p in range(4):
                    n = 4 * t + p
                    if n >= 2:
                        pe.wait_ge(sc_read, 2 * (n - 1))
                    g = p // 2
                    for m in range(2):
                        for r in range(2):
                            j = 4 * g + 2 * (p % 2) + r
                            last = nc.tensor.matmul(ps[:, 2 * (p % 2) + m, r * nk:(r + 1) * nk],
                                                    qT[64 * m:64 * m + 64, j, t * P:(t + 1) * P],
                                                    kT[64 * m:64 * m + 64, g, 0:nk], start=True, stop=True)
                    last.then_inc(sc_done, 1)
                pe.wait_ge(probs_ready, t + 1)
                if t:
                    pe.wait_ge(heads_lo, 4 + 2 * t)

                def weigh(n, f0):
                    pe.wait_ge(pt_out, f0 + n + 1)
                    slot = (f0 + n) % 2
                    for i in range(4 // (t + 1)):
                        h = n * (4 // (t + 1)) + i
                        o = ps[64 * (h % 2):64 * (h % 2) + 64, 6 + h // 8, (h // 2 % 4) * P:(h // 2 % 4 + 1) * P]
                        for c in range(t + 1):
                            last = nc.tensor.matmul(o, kv[:, c, KV_W + HD * (h // 4):KV_W + HD * (h // 4 + 1)],
                                                    pT[:, slot, (i * (t + 1) + c) * P:(i * (t + 1) + c + 1) * P],
                                                    start=(c == 0), stop=(c == t))
                    last.then_inc(pv_done, 1)

                banks = 4 * (t + 1)
                f0 = f
                for n in range(banks):
                    if f >= 2:
                        pe.wait_ge(pt_out, f - 1)
                    for i in range(4):
                        h, c = (4 * n + i, 0) if t == 0 else (2 * n + i // 2, i % 2)
                        last = nc.tensor.transpose(ps[:, 4 + f % 2, i * P:(i + 1) * P],
                                                   probs[:, h, c * P:(c + 1) * P], ident[:])
                    last.then_inc(pt_done, 1)
                    f += 1
                    if n:
                        weigh(n - 1, f0)
                weigh(banks - 1, f0)

            pe.wait_ge(sc_read, 16)
            for b in range(4):
                for i in range(2):
                    t, h = b // 2, 2 * (b % 2) + i
                    last = nc.tensor.matmul(ps[:, b, i * S:(i + 1) * S], qmT[:, h, t * P:(t + 1) * P], kmT[:, h, :],
                                            start=True, stop=True)
                last.then_inc(msc_done, 1)
            pe.wait_ge(probs_ready, T + 1)
            pe.wait_ge(heads_lo, 4 + 2 * T)

            def weigh_mem(n, f0):
                pe.wait_ge(pt_out, f0 + n + 1)
                slot = (f0 + n) % 2
                for i in range(2):
                    t, h = n // 2, 2 * (n % 2) + i
                    for c in range(2):
                        last = nc.tensor.matmul(ps[:, 6 + t, h * P:(h + 1) * P], vm[:, c, h * MHD:(h + 1) * MHD],
                                                pT[:, slot, (2 * i + c) * P:(2 * i + c + 1) * P],
                                                start=(c == 0), stop=(c == 1))
                last.then_inc(pv_done, 1)

            f0 = f
            for n in range(4):
                pe.wait_ge(pt_out, f - 1)
                for i in range(4):
                    last = nc.tensor.transpose(ps[:, 4 + f % 2, i * P:(i + 1) * P],
                                               probs[:, 2 * n + i // 2, (i % 2) * P:(i % 2 + 1) * P], ident[:])
                last.then_inc(pt_done, 1)
                f += 1
                if n:
                    weigh_mem(n - 1, f0)
            weigh_mem(3, f0)

            pe.wait_ge(heads_lo, 3 * T + 4)
            group(OUT0, yT_hi, yT_lo)
            group(OUT1, yT_hi, yT_lo)
            pe.wait_ge(normed, T)
            turn(16, lambda t: resid[:, t, :])
            pe.wait_ge(turned_lo, 24)
            group(PEER0, xT_hi, xT_lo)
            group(PEER1, xT_hi, xT_lo)
            for a in range(2):
                last = nc.tensor.transpose(ps[:, 4, a * P:(a + 1) * P], keys_rows[:, a, :], ident[:])
            last.then_inc(keys_turned, 1)
            pe.wait_ge(evac, n_evac[PEER1 + 1])
            pe.wait_ge(keys_out, 1)
            scT = scores_sb[:]
            for t in range(T):
                for b in range(4):
                    for i in range(4):
                        r = 4 * b + i
                        last = nc.tensor.matmul(ps[:, 4 * (1 - t) + b, i * P:(i + 1) * P],
                                                scT[:, r, t * P:(t + 1) * P], keysT[:, r % 2, :],
                                                start=True, stop=True)
                    last.then_inc(s12_done, 1)

            pe.sem_inc(built, ONES)
            pe.sem_inc(v_used, VSPLIT)
            pe.wait_ge(s12_out, 8)
            for t in range(T):
                pe.wait_ge(weighted, t + 1)
                for a in range(3):
                    src = chosen[:, t, a].rearrange("p h k -> p (h k)") if a < 2 else weight[:, t, :]
                    last = nc.tensor.transpose(ps[:, t, a * P:(a + 1) * P], src, ident[:])
                last.then_inc(pair_turned, 1)
                with pe.Fori(0, P // 16) as i:
                    for k in range(16):
                        n = t * P + k
                        if k % 4 == 0:
                            pe.wait_ge(spread_out, i * 4 + (n // 4 + 1))
                        if k % 8 == 0:
                            pe.wait_ge(hot_key, i * 2 + (n // 8 + 1))
                        pe.wait_ge(hot_weight, i * 16 + (n + 1))
                        nc.tensor.matmul(ps[:, 4 + k // 4, (k % 4) * P:(k % 4 + 1) * P], key_hot[:, k % ONES, :],
                                         weight_hot[:, k % ONES, :], start=True, stop=True).then_inc(built, 1)
            pe.wait_ge(spread_out, 4 + S // 4)

            def blocks(i, first, final):
                for k in range(VRAW):
                    for c in range(DCH):
                        n = DCH * k + c
                        pe.wait_ge(v_lo, i * (VRAW * DCH) + (VRAW * DCH + n + 1))
                        for t in range(T):
                            ah, al = (v[:, k % 2, t * P:(t + 1) * P] for v in (a_hi_sb, a_lo_sb))
                            vh, vl = v_hi_sb[:, n % VSPLIT, :], v_lo_sb[:, n % VSPLIT, :]
                            o = ps[:, DCH * t + c, :]
                            nc.tensor.matmul(o, ah, vh, start=first and k == 0, stop=False)
                            nc.tensor.matmul(o, ah, vl, start=False, stop=False)
                            last = nc.tensor.matmul(o, al, vh, start=False, stop=final and k == VRAW - 1)
                        last.then_inc(v_used, 1)

            turns = BLOCKS // VRAW
            blocks(0, True, False)
            with pe.Fori(1, turns - 1) as i:
                blocks(i, False, False)
            blocks(turns - 1, False, True)


_INS = ["x", "mem", "positions", "w_in", "w_mem_kv", "w_pool", "pool_scale", "attn_sinks", "w_out", "ln1_g", "ln1_b",
        "w_peer_q", "sub_keys_1", "sub_keys_2", "expert_u", "expert_v", "ln2_g", "ln2_b"]


def kernel(**inputs):
    import numpy as np
    import concourse.bacc as bacc
    from concourse.bass_utils import run_bass_kernel_spmd

    nc = bacc.Bacc("TRN2", target_bir_lowering=False, num_devices=1)
    arrays, args = {}, []
    for name in _INS:
        a = np.ascontiguousarray(inputs[name])
        arrays[name] = a
        args.append(nc.dram_tensor(name, a.shape, mybir.dt.from_np(a.dtype), kind="ExternalInput").ap())
    args.append(nc.dram_tensor("out", (1, S, D), F32, kind="ExternalOutput").ap())
    hybrid_layer(nc, *args)
    got = run_bass_kernel_spmd(nc, [arrays], core_ids=[0])
    return got.results[0]["out"]
```

```python
import concourse.bass as bass
from concourse import mybir
from contextlib import ExitStack

F32 = mybir.dt.float32
F32R = mybir.dt.float32r
I32 = mybir.dt.int32
U32 = mybir.dt.uint32
ALU = mybir.AluOpType
ACT = mybir.ActivationFunctionType
AX = mybir.AxisListType

P = 128
D = 2048
S = 256
T = S // P
KC = D // P
POOL_W, SWA_W, KV_W, MEM_W = 512, 1024, 256, 512
WINDOWS = (2, 4, 8, 16)
PAD = WINDOWS[-1]
HEADS, HD = 16, 64
MHEADS, MHD = 4, 128
ROPE = HD // 4
HALF = ROPE // 2
THETA = 500000.0
PHEADS, KEYS, TOPK = 8, 128, 16
PICKS = PHEADS * TOPK
ALPHA = 2.0 ** 0.25
EPS = 1e-5
NEG = -1e30
LOWEST = -3.0e38
PI = 3.14159265358979
ROUND = 12582912.0
TWO_PI = (6.28125, 0.0019350051879882812, 3.0199159819e-07)

COLS = 1024
PAIR = 2
UNITS = KC // PAIR
RAW = 3
SPLIT = 2
RING = 4
PRESET = RING + TOPK
STEPS = 4
STEP_H = PHEADS // STEPS

CH = 512
DCH = 3
DENSE = DCH * CH
TAIL = D - DENSE
BLOCKS = KEYS
VRAW = 4
VSPLIT = 4
VRING = 4
VPRESET = 2 * VRING
KEEP_FREE = 94 * 1024
ONES = 16
HOT = 4

GROUPS = (
    ("q", "RR"),
    ("kv", "R"),
    ("pool_qm", "TT"),
    ("mem", "TR"),
    ("out0", "RR"),
    ("out1", "RR"),
    ("peer0", "TT"),
    ("peer1", "TT"),
)
Q, KV, POOLQM, MEM, OUT0, OUT1, PEER0, PEER1 = range(len(GROUPS))

POOL_U, MEM_U, OUT_U = (UNITS * g for g in (POOLQM, MEM, OUT0))
SCORED = (POOL_U + 2, POOL_U + 4, POOL_U + 6, MEM_U, MEM_U + 3, MEM_U + 5, MEM_U + 7, OUT_U)
BATCHES = len(SCORED)
SWA_BATCHES = 6
LAG = dict(max=2, exp=3, norm=4, turn0=3, copy0=5, turn1=4, copy1=6, sum1=5, out=7)
POOL_TURN = MEM_U + 2
POOL_OUT = MEM_U + 4


def hybrid_layer(nc, x, mem, positions, w_in, w_mem_kv, w_pool, pool_scale, attn_sinks, w_out, ln1_g, ln1_b,
                 w_peer_q, sub_keys_1, sub_keys_2, expert_u, expert_v, ln2_g, ln2_b, out):
    ctx = ExitStack()
    with ctx:
        def sb(name, shape, dt, where=ctx):
            return where.enter_context(nc.sbuf_tensor(name, shape, dt))

        def sem(name):
            return ctx.enter_context(nc.semaphore(name))

        resid = sb("resid", [P, T, D], F32)
        ident = sb("ident", [P, P], F32)
        keysT = sb("keysT", [P, 2, KEYS], F32)
        stats = sb("stats", [P, T, 4, 6], F32)
        moments = sb("moments", [P, T, 2], F32)
        rstd = sb("rstd", [P, 5, T], F32)
        iota = sb("iota", [P, KEYS], F32)
        ps = ctx.enter_context(nc.psum_tensor("ps", [P, 8, 512], F32))

        mix = ExitStack()
        probs = sb("probs", [P, HEADS, S], F32, mix)
        yT_hi = sb("yT_hi", [P, KC, S], F32R, mix)
        yT_lo = sb("yT_lo", [P, KC, S], F32R, mix)
        xT_hi = sb("xT_hi", [P, KC, S], F32R, mix)
        xT_lo = sb("xT_lo", [P, KC, S], F32R, mix)
        raw = sb("raw", [P, RAW, PAIR, COLS], F32, mix)
        w_hi_sb = sb("w_hi_sb", [P, SPLIT, PAIR, COLS], F32R, mix)
        w_lo_sb = sb("w_lo_sb", [P, SPLIT, PAIR, COLS], F32R, mix)
        scores_sb = sb("scores_sb", [P, HEADS, S], F32, mix)
        kv = sb("kv", [P, T, 2 * KV_W], F32, mix)
        qT = sb("qT", [P, HEADS // 2, S], F32, mix)
        kT = sb("kT", [P, 2, S], F32, mix)
        qmT = sb("qmT", [P, MHEADS, S], F32, mix)
        kmT = sb("kmT", [P, MHEADS, S], F32, mix)
        vm = sb("vm", [P, T, MEM_W], F32, mix)
        win_a = sb("win_a", [P, 4, PAD + S], F32, mix)
        pT = sb("pT", [P, 2, 512], F32, mix)
        mask = sb("mask", [P, 2, P], F32, mix)
        scale_sb = sb("scale_sb", [P, 4], F32, mix)
        sinks = sb("sinks", [P, HEADS], F32, mix)
        pos_i = sb("pos_i", [P, T], I32, mix)
        pos_f = sb("pos_f", [P, T], F32, mix)
        ang = sb("ang", [P, 2, T, HALF], F32, mix)
        turns = sb("turns", [P, 2, T, HALF], F32, mix)
        cossin = sb("cossin", [P, 2, T, HALF], F32, mix)
        inv_count = sb("inv_count", [P, PAD], F32, mix)
        edge = sb("edge", [P, PAD], F32, mix)
        row_max = sb("row_max", [P, BATCHES, 8], F32, mix)
        neg_max = sb("neg_max", [P, BATCHES, 8], F32, mix)
        sink_in = sb("sink_in", [P, BATCHES, 8], F32, mix)
        sink_e = sb("sink_e", [P, BATCHES, 8], F32, mix)
        row_sum = sb("row_sum", [P, BATCHES, 8], F32, mix)
        row_inv = sb("row_inv", [P, BATCHES, 8], F32, mix)
        probs_flat = probs[:].rearrange("p h s -> p (h s)")
        keys_rows = probs_flat[:, 0:2 * KEYS].rearrange("p (a k) -> p a k", a=2)
        rt = pT[:, 0, :].rearrange("p (a c) -> p a c", a=4)
        q_rows = probs_flat[:, 0:T * SWA_W].rearrange("p (t c) -> p t c", t=T)
        span = 4 * (PAD + S)
        scores_flat = scores_sb[:].rearrange("p h s -> p (h s)")
        sums = [scores_flat[:, i * span:(i + 1) * span].rearrange("p (g s) -> p g s", g=4) for i in range(2)]
        w_pool_sb = scores_flat[:, 2 * span + 4 * S:2 * span + 4 * S + POOL_W].rearrange("p (g s) -> p g s", g=4)
        means = scores_flat[:, 2 * span:2 * span + 4 * S].rearrange("p (g s) -> p g s", g=4)
        by_bank = lambda v: v[:].rearrange("p (b h) s -> p b (h s)", h=2)
        kmT_banks, qmT_banks, peer_qT = by_bank(kmT), by_bank(qmT), by_bank(scores_sb)
        mix.close()

        peer = ExitStack()
        experts = sb("experts", [P, T, PICKS], I32, peer)
        tails = sb("tails", [P, T, PICKS], I32, peer)
        chosen = sb("chosen", [P, T, 2, PHEADS, TOPK], F32, peer)
        window = sb("window", [P, 2, TOPK], I32, peer)
        tail_window = sb("tail_window", [P, 2, VRING], I32, peer)
        gate = sb("gate", [P, T, PHEADS, TOPK], F32, peer)
        gate_sum = sb("gate_sum", [P, PHEADS], F32, peer)
        hid = sb("hid", [P, T, PICKS], F32, peer)
        weight = sb("weight", [P, T, PICKS], F32, peer)
        part_u = ExitStack()
        pairT = sb("pairT", [P, T, 3, P], F32, part_u)
        hot = sb("hot", [P, 2, ONES, KEYS], F32, part_u)
        rows = [sb(f"rows{i}", [P, D], F32, part_u) for i in range(RING)]
        part_u.close()
        v_lo_sb = sb("v_lo_sb", [P, VSPLIT, CH], F32R, peer)
        a_lo_sb = sb("a_lo_sb", [P, 2, S], F32R, peer)
        a_hi_sb = sb("a_hi_sb", [P, 2, S], F32R, peer)
        v_hi_sb = sb("v_hi_sb", [P, VSPLIT, CH], F32R, peer)
        v_raw = sb("v_raw", [P, VRAW, DENSE], F32, peer)
        tail_rows = [sb(f"tail_rows{i}", [P, TAIL], F32, peer) for i in range(VRING)]
        part_r = ExitStack()
        sb("kept_free", [P, KEEP_FREE // 4], F32, part_r)
        s12 = [sb("s12_0", [P, 2 * PHEADS, KEYS], F32, part_r)]
        left = sb("left", [P, 4 * KEYS], F32, part_r)
        cand = sb("cand", [P, STEP_H, TOPK, TOPK], F32, part_r)
        hit = sb("hit", [P, STEP_H, TOPK, TOPK], F32, part_r)
        top_v = sb("top_v", [P, 2 * STEP_H, TOPK], F32, part_r)
        top_i = sb("top_i", [P, 2 * STEP_H, TOPK], U32, part_r)
        top_if = sb("top_if", [P, 2 * STEP_H, TOPK], F32, part_r)
        best_v = sb("best_v", [P, STEP_H, TOPK], F32, part_r)
        best_p = sb("best_p", [P, STEP_H, TOPK], U32, part_r)
        digits = sb("digits", [P, 2, STEP_H, TOPK], U32, part_r)
        digits_f = sb("digits_f", [P, 2, STEP_H, TOPK], F32, part_r)
        s12.append(sb("s12_1", [P, 2 * PHEADS, KEYS], F32, part_r))
        part_r.close()
        part_a = ExitStack()
        spread = sb("spread", [P, T, KEYS, P], F32, part_a)
        part_a.close()
        gain2 = sb("gain2", [P, 2, D], F32, peer)
        peer.close()

        x_in = [sem(f"x_in{c}") for c in range(2)]
        w_pool_in = sem("w_pool_in")
        mem_in, small_in, gain_in, gain2_in, out_done = (
            sem(n) for n in ("mem_in", "small_in", "gain_in", "gain2_in", "out_done"))
        w_in_sem = [sem(f"w_in{i}") for i in range(RAW)]
        consts = sem("consts")
        turned = sem("turned")
        turned_hi = sem("turned_hi")
        turned_lo = sem("turned_lo")
        w_hi, w_lo, w_used = sem("w_hi"), sem("w_lo"), sem("w_used")
        evac = sem("evac")
        qk_turned, qk_out = sem("qk_turned"), sem("qk_out")
        dve_step = sem("dve_step")
        roped = sem("roped")
        sc_done, sc_read = sem("sc_done"), sem("sc_read")
        max_ready, exp_done, probs_ready = sem("max_ready"), sem("exp_done"), sem("probs_ready")
        pt_done, pt_out, pv_done = sem("pt_done"), sem("pt_out"), sem("pv_done")
        heads_hi, heads_lo = sem("heads_hi"), sem("heads_lo")
        keys_turned, keys_out = sem("keys_turned"), sem("keys_out")
        pooled, pool_done, pool_hi, pool_lo = (sem(n) for n in ("pooled", "pool_done", "pool_hi", "pool_lo"))
        var_ready, std_ready, shift_ready = sem("var_ready"), sem("std_ready"), sem("shift_ready")
        centred, normed = sem("centred"), sem("normed")
        s12_done, s12_out = sem("s12_done"), sem("s12_out")
        routed, gate_in, gate_e = sem("routed"), sem("gate_in"), sem("gate_e")
        window_set = sem("window_set")
        row_in = [sem(f"row_in{i}") for i in range(RING)]
        rows_used = sem("rows_used")
        gelu_done, weighted = sem("gelu_done"), sem("weighted")
        pair_turned, pair_out = sem("pair_turned"), sem("pair_out")
        hot_keys, hot_weights = sem("hot_keys"), sem("hot_weights")
        built = sem("built")
        spread_out = sem("spread_out")
        v_in = [sem(f"v_in{i}") for i in range(VRAW)]
        v_hi = sem("v_hi")
        v_lo = sem("v_lo")
        v_used = sem("v_used")
        tail_in = [sem(f"tail_in{i}") for i in range(VRING)]
        tails_used = sem("tails_used")
        tail_set = sem("tail_set")
        tails_known = sem("tails_known")
        turns_ready, sines = sem("turns_ready"), sem("sines")

        n_evac = [0]
        for _, kinds in GROUPS:
            n_evac.append(n_evac[-1] + 2 * len(kinds))

        def unit_of(g, j):
            return UNITS * g + j

        def at(n, stage):
            sooner = 1 if (n, stage) == (BATCHES - 1, "out") else 0
            return SCORED[n] + LAG[stage] - sooner

        def tile_group(n):
            return (0, n, 0) if n < 2 else (1, (n - 2) // 2, (n - 2) % 2)

        def keys_of(n):
            return P if n < 2 else S

        def prob_slot(n):
            return probs_flat[:, (n % 4) * 1024:(n % 4 + 1) * 1024]

        def head_cols(n, v):
            t, g, r = tile_group(n)
            four = v.rearrange("p (g m r) -> p g m r", g=2, m=2)[:, g]
            return four if t == 0 else four[:, :, 2 * r:2 * r + 2]

        def head_chunks(n, v):
            if n >= SWA_BATCHES:
                t = n - SWA_BATCHES
                return v[:, 12:16, t * P:(t + 1) * P]
            t, g, r = tile_group(n)
            c0 = 4 + 4 * g
            return v[:, c0:c0 + 4, 0:P] if t == 0 else v[:, c0 + r:c0 + r + 3:2, P:2 * P]

        def sum_bank(n):
            return 4 if n == BATCHES - 1 else 7

        def head_sums(n):
            chunks = 2 if 2 <= n < SWA_BATCHES else 4
            return ps[:, sum_bank(n), 0:chunks * P].rearrange("p (c s) -> p c s", c=chunks)

        block = ctx.enter_context(nc.Block())

        @block.sync
        def _(sp):
            for c in range(2):
                cols = slice(c * D // 2, (c + 1) * D // 2)
                sp.dma_start(resid[:, :, cols], x[0, :, cols].rearrange("(t p) d -> p t d", p=P)
                             ).then_inc(x_in[c], 16)

            def source(g, j):
                r0, r1 = j * PAIR * P, (j + 1) * PAIR * P
                name = GROUPS[g][0]

                def piece(w, c0, c1):
                    return w[0, r0:r1, c0:c1].rearrange("(a p) n -> p a n", p=P)
                if name == "q":
                    return [(0, piece(w_in, POOL_W, POOL_W + SWA_W))]
                if name == "kv":
                    return [(0, piece(w_in, POOL_W + SWA_W, POOL_W + SWA_W + 2 * KV_W))]
                if name == "mem":
                    return [(0, piece(w_mem_kv, 0, 2 * MEM_W))]
                if name == "pool_qm":
                    q0 = POOL_W + SWA_W + 2 * KV_W
                    return [(0, piece(w_in, 0, POOL_W)), (POOL_W, piece(w_in, q0, q0 + MEM_W))]
                w = w_out if name.startswith("out") else w_peer_q
                c0 = COLS * int(name[-1])
                return [(0, piece(w, c0, c0 + COLS))]

            for g in range(len(GROUPS)):
                for j in range(UNITS):
                    u = unit_of(g, j)
                    if u >= RAW:
                        sp.wait_ge(w_lo, u - RAW + 1)
                    for c0, src in source(g, j):
                        sp.dma_start(raw[:, u % RAW, :, c0:c0 + src.shape[2]], src).then_inc(w_in_sem[u % RAW], 16)
                    if u == 1:
                        sp.dma_start(scores_flat.rearrange("p (t d) -> p t d", t=T),
                                     mem[0].rearrange("(t p) d -> p t d", p=P)).then_inc(mem_in, 16)
                    if (g, j) == (POOLQM, 0):
                        sp.wait_ge(turned, 16)
                        sp.dma_start(w_pool_sb, w_pool[0].rearrange("g c d -> c g d")).then_inc(w_pool_in, 16)
                    if (g, j) == (OUT1, 1):
                        sp.wait_ge(pt_done, 2 * BATCHES)
                        sp.dma_start(probs_flat[:, 0:D], ln1_g[0:1, :].to_broadcast([P, D])).then_inc(gain_in, 16)
                        sp.dma_start(probs_flat[:, D:2 * D], ln1_b[0:1, :].to_broadcast([P, D])
                                     ).then_inc(gain_in, 16)
            sp.wait_ge(rows_used, PRESET + T * PICKS)
            for part, (b0, b1) in enumerate(((0, 24), (24, BLOCKS // VRAW))):
                with sp.Fori(b0, b1) as i:
                    for k in range(VRAW):
                        sp.wait_ge(v_lo, i * (VRAW * DCH) + DCH * (k + 1))
                        sp.dma_start(v_raw[:, k, :], expert_v[0, bass.ds(i * (VRAW * P) + k * P, P), 0:DENSE]
                                     ).then_inc(v_in[k], 16)
                if part == 0:
                    sp.dma_start(gain2[:, 0, :], ln2_g[0:1, :].to_broadcast([P, D])).then_inc(gain2_in, 16)
                    sp.dma_start(gain2[:, 1, :], ln2_b[0:1, :].to_broadcast([P, D])).then_inc(gain2_in, 16)
            for n in range(2 * T):
                sp.wait_ge(normed, (D // CH) * T + 2 * T * (n // T) + T + n % T + 1)
                t, cols = n % T, slice(n // T * D // 2, (n // T + 1) * D // 2)
                sp.dma_start(out[0, t * P:(t + 1) * P, cols], resid[:, t, cols]).then_inc(out_done, 16)
            sp.wait_ge(out_done, 16 * 2 * T)

        def pieces(g):
            return 2 if GROUPS[g][0] == "pool_qm" else 1

        def landed(u):
            n = 0
            for v in range(u % RAW, u + 1, RAW):
                n += 16 * pieces(v // UNITS)
            return n

        def s12_at(t, b):
            return 4 * (b // 2) + 2 * t + b % 2 + 1

        def s12_bank(t, b):
            return (4 if b < 2 else 0) + 2 * t + b % 2

        def width(g):
            return 512 * len(GROUPS[g][1])

        def q_heads(b):
            return ps[:, b, :].rearrange("p (m r c) -> p r m c", m=2, r=4)

        def q_pairs(b):
            return q_rows[:, b % 2, (b // 2) * 512:(b // 2 + 1) * 512].rearrange("p (r m c) -> p r m c", m=2, r=4)

        @block.gpsimd
        def _(pool):
            nc.gpsimd.memset(ident[:], 0.0).then_inc(consts, 1)
            nc.gpsimd.memset(mask[:], 0.0).then_inc(consts, 1)
            nc.gpsimd.memset(win_a[:], 0.0).then_inc(consts, 1)
            pool.wait_ge(consts, 3)
            nc.gpsimd.affine_select(out=ident[:], in_=ident[:], compare_op=ALU.not_equal, fill=1.0, base=0,
                                    pattern=[[-1, P]], channel_multiplier=1).then_inc(consts, 1)
            nc.gpsimd.affine_select(out=mask[:, 0, :], in_=mask[:, 0, :], compare_op=ALU.is_gt, fill=NEG, base=0,
                                    pattern=[[1, P]], channel_multiplier=-1).then_inc(consts, 1)
            nc.gpsimd.affine_select(out=mask[:, 1, :], in_=mask[:, 1, :], compare_op=ALU.is_ge, fill=NEG, base=0,
                                    pattern=[[-1, P]], channel_multiplier=1).then_inc(consts, 1)
            nc.gpsimd.iota(iota[:], [[1, KEYS]], base=0, channel_multiplier=0,
                           allow_small_or_imprecise_dtypes=True).then_inc(consts, 1)
            nc.gpsimd.iota(inv_count[:], [[1, PAD]], base=1, channel_multiplier=0,
                           allow_small_or_imprecise_dtypes=True).then_inc(consts, 1)

            def weigh_rows(t, i, k):
                nc.gpsimd.tensor_tensor(
                    hot[:, 0, k % ONES:k % ONES + HOT, :], hot[:, 0, k % ONES:k % ONES + HOT, :],
                    pairT[:, t, 2, bass.ds(i + k, HOT)].unsqueeze(2).to_broadcast([P, HOT, KEYS]), ALU.mult
                ).then_inc(hot_weights, 1)

            pool.wait_ge(w_used, unit_of(len(GROUPS), 0))
            for t in range(T):
                first = t * PICKS
                with pool.Fori(0, PHEADS // 2) as i:
                    pool.wait_ge(routed, i + (STEPS * t + 1))
                    for half in range(2):
                        pool.wait_ge(rows_used, i * (2 * TOPK) + (first + half * TOPK + RING))
                        nc.gpsimd.tensor_copy(window[:, half, :],
                                              experts[:, t, bass.ds(i * (2 * TOPK) + half * TOPK, TOPK)]
                                              ).then_inc(window_set, 1)
                        pool.wait_ge(window_set, i * 2 + (t * PHEADS + half + 1))
                        for k in range(TOPK):
                            pool.wait_ge(rows_used, i * (2 * TOPK) + (first + half * TOPK + k + 1 + TOPK))
                            pool.nop(nofuse=True)
                            nc.gpsimd.indirect_dma_start(
                                rows[k % RING][:], None, expert_u[0],
                                bass.IndirectOffsetOnAxis(ap=window[:, half, k:k + 1], axis=0)
                            ).then_inc(row_in[k % RING], 16)
                            if t and k % HOT == HOT - 1:
                                n = half * TOPK + k + 1 - HOT
                                pool.wait_ge(hot_keys, i * (2 * TOPK // HOT) + (n // HOT + 1))
                                pool.nop(nofuse=True)
                                weigh_rows(0, i * (2 * TOPK), n)
            with pool.Fori(0, PHEADS) as i:
                for k in range(0, TOPK, HOT):
                    pool.wait_ge(hot_keys, i * (TOPK // HOT) + ((P + k) // HOT + 1))
                    pool.nop(nofuse=True)
                    weigh_rows(1, i * TOPK, k)
            tail_table = expert_v[0].rearrange("e (c n) -> (e c) n", n=TAIL)
            pool.wait_ge(tails_known, T)
            pool.wait_ge(rows_used, PRESET + T * PICKS)
            for t in range(T):
                with pool.Fori(0, PICKS // (2 * VRING)) as i:
                    for half in range(2):
                        n0 = t * PICKS + half * VRING
                        pool.wait_ge(tails_used, i * (2 * VRING) + (n0 + VRING))
                        nc.gpsimd.tensor_copy(tail_window[:, half, :],
                                              tails[:, t, bass.ds(i * (2 * VRING) + half * VRING, VRING)]
                                              ).then_inc(tail_set, 1)
                        pool.wait_ge(tail_set, i * 2 + (2 * t * (PICKS // (2 * VRING)) + half + 1))
                        for k in range(VRING):
                            pool.wait_ge(tails_used, i * (2 * VRING) + (n0 + k + 1 + VRING))
                            pool.nop(nofuse=True)
                            nc.gpsimd.indirect_dma_start(
                                tail_rows[k][:], None, tail_table,
                                bass.IndirectOffsetOnAxis(ap=tail_window[:, half, k:k + 1], axis=0)
                            ).then_inc(tail_in[k], 16)

        @block.scalar
        def _(act):
            act.dma_start(pos_i[:], positions[0].rearrange("(t p) -> p t", p=P),
                          allow_slow_non_contiguous=True).then_inc(small_in, 16)
            act.dma_start(scale_sb[:], pool_scale[0].rearrange("(c p) -> p c", p=P),
                          allow_slow_non_contiguous=True).then_inc(small_in, 16)
            act.dma_start(sinks[:], attn_sinks[0:1, :].to_broadcast([P, HEADS])).then_inc(small_in, 16)
            act.dma_start(keys_rows[:, 0, :], sub_keys_1[0]).then_inc(small_in, 16)
            act.dma_start(keys_rows[:, 1, :], sub_keys_2[0]).then_inc(small_in, 16)

            def turn_out(first, b, dst):
                act.wait_ge(turned, first + b + 1)
                nc.scalar.activation(dst[:, 2 * b:2 * b + 2, :].rearrange("p a s -> p (a s)"),
                                     ps[:, 4 + b % 4, :], ACT.Copy).then_inc(turned_hi, 1)

            def split(g, j):
                u = unit_of(g, j)
                act.wait_ge(w_in_sem[u % RAW], landed(u))
                if u >= SPLIT:
                    act.wait_ge(w_used, u - SPLIT + 1)
                nc.scalar.activation(w_hi_sb[:, u % SPLIT, :, 0:width(g)], raw[:, u % RAW, :, 0:width(g)],
                                     ACT.Copy).then_inc(w_hi, 1)

            def read_out(g, banks, dst):
                act.wait_ge(w_used, unit_of(g, UNITS))
                for b in banks:
                    nc.scalar.activation(dst(b), ps[:, b, :], ACT.Copy).then_inc(evac, 1)

            def attend(u):
                for n in range(BATCHES):
                    if u == at(n, "exp"):
                        act.wait_ge(max_ready, n + 1)
                        nk, probs_n = keys_of(n), prob_slot(n)
                        for h in range(1024 // nk):
                            of_head = probs_n[:, h * nk:(h + 1) * nk]
                            last = nc.scalar.activation(of_head, of_head, ACT.Exp, bias=neg_max[:, n, h:h + 1],
                                                        accum_out=row_sum[:, n, h:h + 1])
                        if n < SWA_BATCHES:
                            heads = slice(0, 1024 // nk)
                            last = nc.scalar.activation(sink_e[:, n, heads], sink_in[:, n, heads], ACT.Exp)
                        last.then_inc(exp_done, 1)
                    for half in range(2):
                        if u == at(n, f"copy{half}"):
                            f = 2 * n + half
                            act.wait_ge(pt_done, f + 1)
                            if f >= 2:
                                act.wait_ge(pv_done, f - 1)
                            nc.scalar.activation(pT[:, f % 2, :], ps[:, 6, :], ACT.Copy).then_inc(pt_out, 1)
                    if u == at(n, "out"):
                        act.wait_ge(pv_done, 2 * n + 2)
                        nc.scalar.activation(head_chunks(n, xT_hi), head_sums(n), ACT.Copy).then_inc(heads_hi, 1)

            def between(g, j):
                u = unit_of(g, j)
                if (g, j) == (KV, 0):
                    act.wait_ge(w_used, unit_of(Q, UNITS))
                    for b in (0, 2):
                        nc.scalar.activation(q_pairs(b), q_heads(b), ACT.Copy).then_inc(evac, 1)
                if 2 <= u < 10:
                    turn_out(8, u - 2, yT_hi)
                if (g, j) == (Q, 3):
                    act.wait_ge(turns_ready, 1)
                    nc.scalar.activation(cossin[:], ang[:], ACT.Sin).then_inc(sines, 1)
                if (g, j) == (Q, 1):
                    act.wait_ge(keys_turned, 1)
                    nc.scalar.activation(keysT[:].rearrange("p a k -> p (a k)"), ps[:, 7, 0:2 * KEYS], ACT.Copy
                                         ).then_inc(keys_out, 1)
                if (g, j) == (POOLQM, 0):
                    read_out(KV, (0,), lambda b: kv[:, b, :])
                if g == POOLQM and j < 3:
                    for i in ((0, 1), (2, 3), (4,))[j]:
                        act.wait_ge(qk_turned, i + 1)
                        dst = qT[:, 2 * i:2 * i + 2, :] if i < 4 else kT[:]
                        nc.scalar.activation(dst.rearrange("p a s -> p (a s)"), ps[:, 4 + i % 4, :], ACT.Copy
                                             ).then_inc(qk_out, 1)
                if (g, j) == (MEM, 0):
                    read_out(POOLQM, (2, 3), lambda b: qmT_banks[:, b - 2, :])
                if u == POOL_OUT:
                    act.wait_ge(pool_done, 1)
                    for i in range(4):
                        nc.scalar.activation(xT_hi[:, i, :], ps[:, 4 + i // 2, (i % 2) * S:(i % 2 + 1) * S], ACT.Copy,
                                             scale=scale_sb[:, i:i + 1]).then_inc(pool_hi, 1)
                if (g, j) == (OUT0, 0):
                    read_out(MEM, (0, 2), lambda b: kmT_banks[:, b, :] if b < 2 else vm[:, b - 2, :])
                attend(u)
                if (g, j) == (PEER0, 1):
                    centre(0)
                    for b in range(KC // 2):
                        turn_out(16, b, yT_hi)
                if (g, j) == (PEER1, 0):
                    read_out(PEER0, (0, 2), lambda b: peer_qT[:, b, :])
                if (g, j) == (PEER1, 2):
                    scores_out(0, range(2))

            def centre(n):
                act.wait_ge(var_ready, n + 1)
                nc.scalar.activation(rstd[:, 0, :], rstd[:, 1, :], ACT.Sqrt).then_inc(std_ready, 1)
                act.wait_ge(shift_ready, n + 1)
                for c in range(D // CH):
                    for t in range(T):
                        cols = resid[:, t, c * CH:(c + 1) * CH]
                        nc.scalar.activation(cols, cols, ACT.Identity, bias=rstd[:, 4, t:t + 1],
                                             scale=rstd[:, 2, t:t + 1]).then_inc(centred, 1)

            def scores_out(t, banks):
                for b in banks:
                    act.wait_ge(s12_done, s12_at(t, b))
                    nc.scalar.activation(s12[t][:, 4 * b:4 * b + 4, :].rearrange("p a s -> p (a s)"),
                                         ps[:, s12_bank(t, b), :], ACT.Copy).then_inc(s12_out, 1)

            for b in range(4):
                turn_out(0, b, xT_hi)
            for g in range(len(GROUPS)):
                for j in range(UNITS):
                    split(g, j)
                    if (g, j) == (Q, 0):
                        for b in range(4, KC // 2):
                            turn_out(0, b, xT_hi)
                    between(g, j)
            read_out(PEER1, (0, 2), lambda b: peer_qT[:, 4 + b, :])
            act.sem_inc(spread_out, 4)
            scores_out(0, range(2, 4))
            scores_out(1, range(4))
            for t in range(T):
                act.wait_ge(gate_in, STEPS * (t + 1))
                nc.scalar.activation(gate[:, t], gate[:, t], ACT.Exp).then_inc(gate_e, 1)
                act.wait_ge(rows_used, PRESET + (t + 1) * PICKS)
                nc.scalar.activation(weight[:, t, :], hid[:, t, :], ACT.Gelu).then_inc(gelu_done, 1)
                act.wait_ge(pair_turned, t + 1)
                nc.scalar.activation(pairT[:, t].rearrange("p a s -> p (a s)"), ps[:, t, 0:3 * P], ACT.Copy
                                     ).then_inc(pair_out, 1)
                with act.Fori(0, P // 16) as i:
                    for q in range(4):
                        act.wait_ge(built, i * 16 + (ONES + P * t + 4 * q + 4))
                        act.nop(nofuse=True)
                        nc.scalar.activation(
                            spread[:, t, :, bass.ds(i * 16 + 4 * q, 4)].rearrange("p k s -> p s k"),
                            ps[:, 4 + q, :].rearrange("p (s k) -> p s k", s=4), ACT.Copy).then_inc(spread_out, 1)

            act.wait_ge(spread_out, 4 + S // 4)
            with act.Fori(0, BLOCKS // VRAW) as i:
                for k in range(VRAW):
                    act.wait_ge(v_used, i * (VRAW * DCH) + (DCH * k + 1))
                    act.nop(nofuse=True)
                    nc.scalar.activation(a_hi_sb[:, k % 2, :].rearrange("p (t a s) -> p t a s", t=T, a=1),
                                         spread[:, :, bass.ds(i * VRAW + k, 1), :], ACT.Copy).then_inc(v_hi, 1)
                    act.wait_ge(v_in[k], i * 16 + 16)
                    for c in range(DCH):
                        act.wait_ge(v_used, i * (VRAW * DCH) + (DCH * k + c + 1))
                        nc.scalar.activation(v_hi_sb[:, (DCH * k + c) % VSPLIT, :],
                                             v_raw[:, k, c * CH:(c + 1) * CH], ACT.Copy).then_inc(v_hi, 1)
            centre(1)

        @block.vector
        def _(dve):
            steps = [0]

            def link(ins):
                steps[0] += 1
                ins.then_inc(dve_step, 1)
                dve.wait_ge(dve_step, steps[0])

            def turn_low(first, b, hi, lo):
                dve.wait_ge(turned_hi, first + b + 1)
                nc.vector.tensor_tensor(lo[:, 2 * b:2 * b + 2, :].rearrange("p a s -> p (a s)"),
                                        ps[:, 4 + b % 4, :],
                                        hi[:, 2 * b:2 * b + 2, :].rearrange("p a s -> p (a s)").bitcast(F32),
                                        ALU.subtract).then_inc(turned_lo, 1)

            def split(g, j):
                u = unit_of(g, j)
                dve.wait_ge(w_hi, u + 1)
                nc.vector.tensor_tensor(w_lo_sb[:, u % SPLIT, :, 0:width(g)], raw[:, u % RAW, :, 0:width(g)],
                                        w_hi_sb[:, u % SPLIT, :, 0:width(g)].bitcast(F32),
                                        ALU.subtract).then_inc(w_lo, 1)

            def read_out(g, banks, dst):
                dve.wait_ge(w_used, unit_of(g, UNITS))
                for b in banks:
                    nc.vector.tensor_copy(dst(b), ps[:, b, :]).then_inc(evac, 1)

            def angles():
                dve.wait_ge(small_in, 16 * 5)
                link(nc.vector.tensor_copy(pos_f[:], pos_i[:]))
                for j in range(HALF):
                    last = nc.vector.tensor_scalar(ang[:, 1, :, j], pos_f[:], float(THETA ** (-2.0 * j / ROPE)), None,
                                                   ALU.mult)
                link(last)
                link(nc.vector.tensor_scalar(ang[:, 0], ang[:, 1], PI / 2, None, ALU.add))
                link(nc.vector.tensor_scalar(turns[:], ang[:], 0.5 / PI, ROUND, ALU.mult, ALU.add))
                link(nc.vector.tensor_scalar(turns[:], turns[:], ROUND, None, ALU.subtract))
                for part in TWO_PI:
                    link(nc.vector.scalar_tensor_tensor(out=ang[:], in0=turns[:], scalar=-part, in1=ang[:],
                                                        op0=ALU.mult, op1=ALU.add))
                nc.vector.tensor_scalar(ang[:], ang[:], -3.1415925, 3.1415925, ALU.max, ALU.min
                                        ).then_inc(turns_ready, 1)
                dve.wait_ge(consts, 8)
                link(nc.vector.reciprocal(inv_count[:], inv_count[:]))

            def rotate(t, *parts):
                for rows_, heads_n, done in parts:
                    heads = rows_.rearrange("p (h c) -> p h c", c=HD)
                    a, b = heads[:, :, 0:HALF], heads[:, :, HALF:ROPE]
                    cos = cossin[:, 0, t, :].unsqueeze(1).to_broadcast([P, heads_n, HALF])
                    sin = cossin[:, 1, t, :].unsqueeze(1).to_broadcast([P, heads_n, HALF])
                    r = [rt[:, k, 0:heads_n * HALF].rearrange("p (h c) -> p h c", c=HALF) for k in range(4)]
                    nc.vector.tensor_tensor(r[0], a, cos, ALU.mult)
                    nc.vector.tensor_tensor(r[1], b, sin, ALU.mult)
                    nc.vector.tensor_tensor(r[2], b, cos, ALU.mult)
                    link(nc.vector.tensor_tensor(r[3], a, sin, ALU.mult))
                    nc.vector.tensor_tensor(a, r[0], r[1], ALU.subtract)
                    nc.vector.tensor_tensor(b, r[2], r[3], ALU.add).then_inc(roped, 1)
                    dve.wait_ge(roped, done)

            def window_sums(levels):
                for lev in levels:
                    src, dst = (sums[(lev - 1) % 2] if lev else win_a), sums[lev % 2]
                    back, w = 1 << lev, WINDOWS[lev]
                    nc.vector.tensor_scalar(edge[:, 0:w], inv_count[:, 0:w], float(w), None, ALU.mult)
                    link(nc.vector.tensor_tensor(dst[:, lev:4, PAD:], src[:, lev:4, PAD:],
                                                 src[:, lev:4, PAD - back:PAD + S - back], ALU.add))
                    link(nc.vector.tensor_tensor(dst[:, lev, PAD:PAD + w], dst[:, lev, PAD:PAD + w], edge[:, 0:w],
                                                 ALU.mult))
                    nc.vector.scalar_tensor_tensor(out=means[:, lev, :], in0=dst[:, lev, PAD:], scalar=1.0 / w,
                                                   in1=win_a[:, lev, PAD:], op0=ALU.mult, op1=ALU.subtract
                                                   ).then_inc(pooled, 1)
                    dve.wait_ge(pooled, lev + 1)

            def attend(u):
                for n in range(BATCHES):
                    nk = keys_of(n)
                    heads = 1024 // nk
                    by_head = prob_slot(n).rearrange("p (h s) -> p h s", h=heads)
                    if u == at(n, "max"):
                        dve.wait_ge(sc_done, n + 1)
                        if n < SWA_BATCHES:
                            t = tile_group(n)[0]
                            mk = mask[:, 1 - t:2, :].rearrange("p a s -> p (a s)").unsqueeze(1).to_broadcast(
                                [P, heads // 2, nk])
                            for m in range(2):
                                last = nc.vector.scalar_tensor_tensor(
                                    out=by_head[:, m * heads // 2:(m + 1) * heads // 2, :],
                                    in0=ps[:, 4 + m, :].rearrange("p (h s) -> p h s", h=heads // 2),
                                    scalar=float(HD) ** -0.5, in1=mk, op0=ALU.mult, op1=ALU.add)
                        else:
                            for m in range(2):
                                last = nc.vector.tensor_scalar(prob_slot(n)[:, m * 512:(m + 1) * 512],
                                                               ps[:, 4 + m, :], float(MHD) ** -0.5, None, ALU.mult)
                        last.then_inc(sc_read, 1)
                        dve.wait_ge(sc_read, n + 1)
                        link(nc.vector.reduce_max(row_max[:, n, 0:heads], by_head, AX.X))
                        if n < SWA_BATCHES:
                            mx, sink = row_max[:, n, 0:heads].rearrange("p (m r) -> p m r", m=2), head_cols(n, sinks[:])
                            link(nc.vector.tensor_tensor(mx, mx, sink, ALU.max))
                            nc.vector.tensor_tensor(sink_in[:, n, 0:heads].rearrange("p (m r) -> p m r", m=2),
                                                    sink, mx, ALU.subtract)
                        nc.vector.tensor_scalar(neg_max[:, n, 0:heads], row_max[:, n, 0:heads], -1.0, None, ALU.mult
                                                ).then_inc(max_ready, 1)
                    if u == at(n, "norm"):
                        dve.wait_ge(exp_done, n + 1)
                        total = row_sum[:, n, 0:heads]
                        if n < SWA_BATCHES:
                            link(nc.vector.tensor_tensor(total, total, sink_e[:, n, 0:heads], ALU.add))
                        link(nc.vector.reciprocal(row_inv[:, n, 0:heads], total))
                        nc.vector.tensor_tensor(by_head, by_head,
                                                row_inv[:, n, 0:heads].unsqueeze(2).to_broadcast([P, heads, nk]),
                                                ALU.mult).then_inc(probs_ready, 1)
                    if u == at(n, "out"):
                        dve.wait_ge(heads_hi, n + 1)
                        nc.vector.tensor_tensor(head_chunks(n, xT_lo), head_sums(n),
                                                head_chunks(n, xT_hi).bitcast(F32), ALU.subtract
                                                ).then_inc(heads_lo, 1)

            def add_residual(g):
                dve.wait_ge(w_used, unit_of(g, UNITS))
                for b in range(4):
                    c0 = COLS * (g - OUT0) + 512 * (b // 2)
                    cols = resid[:, b % 2, c0:c0 + 512]
                    nc.vector.scalar_tensor_tensor(out=cols, in0=cols, scalar=ALPHA, in1=ps[:, b, :],
                                                   op0=ALU.mult, op1=ALU.add).then_inc(evac, 1)

            def row_stats(banks):
                for c in banks:
                    for t in range(T):
                        last = nc.vector.bn_stats(stats[:, t, c, :], resid[:, t, 512 * c:512 * (c + 1)])
                link(last)

            def norm(n, gain, shift):
                for t in range(T):
                    last = nc.vector.bn_aggr(moments[:, t, :], stats[:, t].rearrange("p c k -> p (c k)"))
                link(last)
                nc.vector.tensor_scalar(rstd[:, 1, :], moments[:, :, 1], EPS, None, ALU.add).then_inc(var_ready, 1)
                dve.wait_ge(std_ready, n + 1)
                link(nc.vector.reciprocal(rstd[:, 2, :], rstd[:, 0, :]))
                link(nc.vector.tensor_tensor(rstd[:, 3, :], rstd[:, 2, :], rstd[:, 2, :], ALU.mult))
                link(nc.vector.tensor_tensor(rstd[:, 3, :], rstd[:, 3, :], rstd[:, 1, :], ALU.mult))
                link(nc.vector.tensor_scalar(rstd[:, 3, :], rstd[:, 3, :], -0.5, 1.5, ALU.mult, ALU.add))
                link(nc.vector.tensor_tensor(rstd[:, 2, :], rstd[:, 2, :], rstd[:, 3, :], ALU.mult))
                nc.vector.scalar_tensor_tensor(out=rstd[:, 4, :], in0=moments[:, :, 0], scalar=-1.0,
                                               in1=rstd[:, 2, :], op0=ALU.mult, op1=ALU.mult
                                               ).then_inc(shift_ready, 1)
                for c in range(D // CH):
                    for t in range(T):
                        cols = slice(c * CH, (c + 1) * CH)
                        tile = resid[:, t, cols]
                        dve.wait_ge(centred, (D // CH) * T * n + T * c + t + 1)
                        link(nc.vector.tensor_tensor(tile, tile, gain[:, cols], ALU.mult))
                        nc.vector.tensor_tensor(tile, tile, shift[:, cols], ALU.add).then_inc(normed, 1)

            def between(g, j):
                u = unit_of(g, j)
                if (g, j) == (Q, 0):
                    angles()
                if (g, j) == (KV, 0):
                    dve.wait_ge(w_used, unit_of(Q, UNITS))
                    for b in (1, 3):
                        nc.vector.tensor_copy(q_pairs(b), q_heads(b)).then_inc(evac, 1)
                if 2 <= u < 10:
                    turn_low(8, u - 2, yT_hi, yT_lo)
                if g == KV and j in (2, 4):
                    dve.wait_ge(sines, 1)
                    dve.wait_ge(evac, n_evac[KV])
                    t = j // 2 - 1
                    rotate(t, (q_rows[:, t, :], HEADS, t + 1))
                if (g, j) == (POOLQM, 0):
                    read_out(KV, (1,), lambda b: kv[:, b, :])
                    dve.wait_ge(evac, n_evac[KV + 1])
                    for t in range(T):
                        rotate(t, (kv[:, t, 0:KV_W], KV_W // HD, T + t + 1))
                if (g, j) == (MEM, 0):
                    dve.wait_ge(w_used, unit_of(POOLQM, UNITS))
                    for b in (0, 1):
                        nc.vector.tensor_copy(win_a[:, 2 * b:2 * b + 2, PAD:],
                                              ps[:, b, :].rearrange("p (g s) -> p g s", g=2)).then_inc(evac, 1)
                    for dst in sums:
                        nc.vector.memset(dst[:, :, 0:PAD], 0.0)
                    dve.wait_ge(evac, n_evac[POOLQM + 1])
                if (g, j) == (MEM, 1):
                    window_sums((0, 1))
                if (g, j) == (MEM, 2):
                    window_sums((2, 3))
                if u == POOL_OUT:
                    for i in range(4):
                        dve.wait_ge(pool_hi, 2 * (i // 2) + 2)
                        nc.vector.scalar_tensor_tensor(out=xT_lo[:, i, :],
                                                       in0=ps[:, 4 + i // 2, (i % 2) * S:(i % 2 + 1) * S],
                                                       scalar=scale_sb[:, i:i + 1], in1=xT_hi[:, i, :].bitcast(F32),
                                                       op0=ALU.mult, op1=ALU.subtract).then_inc(pool_lo, 1)
                if (g, j) == (OUT0, 0):
                    read_out(MEM, (1, 3), lambda b: kmT_banks[:, b, :] if b < 2 else vm[:, b - 2, :])
                attend(u)
                if (g, j) == (OUT1, 0):
                    add_residual(OUT0)
                if (g, j) == (OUT1, 2):
                    dve.wait_ge(evac, n_evac[OUT0 + 1])
                    row_stats((0, 1))
                if (g, j) == (PEER0, 0):
                    add_residual(OUT1)
                    dve.wait_ge(evac, n_evac[OUT1 + 1])
                    dve.wait_ge(gain_in, 32)
                    row_stats((2, 3))
                    norm(0, probs_flat[:, 0:D], probs_flat[:, D:2 * D])
                    for b in range(KC // 2):
                        turn_low(16, b, yT_hi, yT_lo)
                if (g, j) == (PEER1, 0):
                    read_out(PEER0, (1, 3), lambda b: peer_qT[:, b, :])
                if (g, j) == (PEER1, 3):
                    route(0, 0)
                if (g, j) == (PEER1, 5):
                    best(0, 0)
                if (g, j) == (PEER1, 7):
                    choose(0, 0)

            def top16(n, values, rest, best, index):
                for r in range(n):
                    last = nc.vector.max(best(r)[:, 0:8], values(r))
                link(last)
                for r in range(n):
                    last = nc.vector.match_replace(rest(r), best(r)[:, 0:8], values(r), LOWEST)
                link(last)
                for r in range(n):
                    last = nc.vector.max(best(r)[:, 8:16], rest(r))
                link(last)
                for r in range(n):
                    nc.vector.max_index(index(r)[:, 0:8], best(r)[:, 0:8], values(r))
                    last = nc.vector.max_index(index(r)[:, 8:16], best(r)[:, 8:16], rest(r))
                link(last)

            def route(t, step):
                dve.wait_ge(s12_out, STEPS * t + step + 1)
                left3 = left[:].rearrange("p (r k) -> p r k", k=KEYS)
                top16(2 * STEP_H, lambda r: s12[t][:, 2 * STEP_H * step + r, :], lambda r: left3[:, r, :],
                      lambda r: top_v[:, r, :], lambda r: top_i[:, r, :])
                nc.vector.tensor_copy(top_if[:], top_i[:])
                tv = top_v[:].rearrange("p (h a) k -> p h a k", a=2)
                wide = [P, STEP_H, TOPK, TOPK]
                link(nc.vector.tensor_tensor(cand[:], tv[:, :, 0, :].unsqueeze(3).to_broadcast(wide),
                                             tv[:, :, 1, :].unsqueeze(2).to_broadcast(wide), ALU.add))

            def best(t, step):
                heads = slice(STEP_H * step, STEP_H * (step + 1))
                left4 = left[:].rearrange("p (h k) -> p h k", k=TOPK * TOPK)
                top16(STEP_H, lambda h: cand[:, h].rearrange("p a b -> p (a b)"), lambda h: left4[:, h, :],
                      lambda h: best_v[:, h, :], lambda h: best_p[:, h, :])
                nc.vector.tensor_tensor(gate[:, t, heads], best_v[:],
                                        best_v[:, :, 0:1].to_broadcast([P, STEP_H, TOPK]),
                                        ALU.subtract).then_inc(gate_in, 1)

            def choose(t, step):
                heads = slice(STEP_H * step, STEP_H * (step + 1))
                wide = [P, STEP_H, TOPK, TOPK]
                nc.vector.tensor_scalar(digits[:, 0], best_p[:], 4, None, ALU.logical_shift_right)
                link(nc.vector.tensor_scalar(digits[:, 1], best_p[:], TOPK - 1, None, ALU.bitwise_and))
                link(nc.vector.tensor_copy(digits_f[:], digits[:]))
                tif = top_if[:].rearrange("p (h a) k -> p h a k", a=2)
                for a in range(2):
                    link(nc.vector.tensor_tensor(
                        hit[:], digits_f[:, a].unsqueeze(3).to_broadcast(wide),
                        iota[:, 0:TOPK].unsqueeze(1).unsqueeze(1).to_broadcast(wide), ALU.is_equal))
                    link(nc.vector.tensor_tensor(
                        hit[:], hit[:], tif[:, :, a, :].unsqueeze(2).to_broadcast(wide), ALU.mult))
                    link(nc.vector.reduce_sum(chosen[:, t, a, heads], hit[:], AX.X))
                picks = experts[:, t, :].rearrange("p (h k) -> p h k", h=PHEADS)[:, heads]
                nc.vector.scalar_tensor_tensor(out=picks, in0=chosen[:, t, 0, heads],
                                               scalar=float(KEYS), in1=chosen[:, t, 1, heads],
                                               op0=ALU.mult, op1=ALU.add).then_inc(routed, 1)

            def tails_of(t):
                first_key, second = (chosen[:, t, a].rearrange("p h k -> p (h k)") for a in range(2))
                expert = left[:, t * PICKS:(t + 1) * PICKS]
                link(nc.vector.scalar_tensor_tensor(out=expert, in0=first_key, scalar=float(KEYS), in1=second,
                                                    op0=ALU.mult, op1=ALU.add))
                nc.vector.tensor_scalar(tails[:, t, :], expert, float(D // TAIL), float(D // TAIL - 1),
                                        ALU.mult, ALU.add).then_inc(tails_known, 1)

            def gathered(i, first, k):
                dve.wait_ge(row_in[k % RING], i * (16 * TOPK // RING) + 16 * ((first + k) // RING + 1))

            def hidden(t, k, col):
                unit_ = hid[:, t, col:col + 1] if isinstance(col, int) else hid[:, t, bass.ds(col, 1)]
                nc.vector.scalar_tensor_tensor(
                    out=rows[k % RING][:], in0=rows[k % RING][:], scalar=1.0, in1=resid[:, t, :],
                    op0=ALU.mult, op1=ALU.mult, accum_out=unit_).then_inc(rows_used, 1)

            def weights(t):
                dve.wait_ge(gate_e, t + 1)
                link(nc.vector.reduce_sum(gate_sum[:], gate[:, t], AX.X))
                link(nc.vector.reciprocal(gate_sum[:], gate_sum[:]))
                link(nc.vector.tensor_tensor(gate[:, t], gate[:, t],
                                             gate_sum[:].unsqueeze(2).to_broadcast([P, PHEADS, TOPK]), ALU.mult))
                dve.wait_ge(gelu_done, t + 1)
                nc.vector.tensor_tensor(weight[:, t, :], weight[:, t, :], gate[:, t].rearrange("p h k -> p (h k)"),
                                        ALU.mult).then_inc(weighted, 1)

            def one_hot(i, t, k):
                dve.wait_ge(built, i * TOPK + (t * P + k + HOT))
                both = [P, 2, HOT, KEYS]
                nc.vector.tensor_tensor(
                    hot[:, :, k:k + HOT, :], iota[:].unsqueeze(1).unsqueeze(1).to_broadcast(both),
                    pairT[:, t, 0:2, bass.ds(i * TOPK + k, HOT)].unsqueeze(3).to_broadcast(both),
                    ALU.is_equal).then_inc(hot_keys, 1)

            dve.sem_inc(rows_used, PRESET)
            dve.sem_inc(v_lo, VRAW * DCH)
            dve.sem_inc(tails_used, VPRESET)
            for b in range(4):
                turn_low(0, b, xT_hi, xT_lo)
            for g in range(len(GROUPS)):
                for j in range(UNITS):
                    split(g, j)
                    if (g, j) == (Q, 0):
                        for b in range(4, KC // 2):
                            turn_low(0, b, xT_hi, xT_lo)
                    between(g, j)
            read_out(PEER1, (1, 3), lambda b: peer_qT[:, 4 + b, :])

            quarters = PICKS // RING
            parts = [(part, t, step) for t in range(T) for step in range(STEPS) for part in (route, best, choose)][3:]
            parts, late = parts[:-5], parts[-5:]
            for n in range(quarters):
                for k in range(RING):
                    dve.wait_ge(row_in[k], 16 * (n + 1))
                    hidden(0, k, n * RING + k)
                for part, t, step in parts[n * len(parts) // quarters:(n + 1) * len(parts) // quarters]:
                    part(t, step)
            tails_of(0)
            weights(0)
            dve.wait_ge(pair_out, 1)
            for h in range(len(late) + 1):
                with dve.Fori(h, h + 1 if h < len(late) else PHEADS) as i:
                    for k in range(TOPK):
                        if k % HOT == 0:
                            one_hot(i, 0, k)
                        gathered(i, PICKS, k)
                        hidden(1, k, i * TOPK + k)
                if h < len(late):
                    part, t, step = late[h]
                    part(t, step)
            weights(1)
            tails_of(1)
            dve.wait_ge(rows_used, PRESET + T * PICKS)
            link(nc.vector.tensor_scalar(resid[:, :, DENSE:], resid[:, :, DENSE:], ALPHA, None, ALU.mult))
            dve.wait_ge(pair_out, 2)
            with dve.Fori(0, PHEADS) as i:
                for k in range(0, TOPK, HOT):
                    one_hot(i, 1, k)
            dve.wait_ge(built, ONES + S)
            dve.wait_ge(spread_out, 4 + S // 4)
            half = BLOCKS // VRAW // T
            for t in range(T):
                with dve.Fori(0, half) as i:
                    for k in range(VRAW):
                        b = VRAW * half * t + k
                        dve.wait_ge(v_hi, i * (VRAW * (DCH + 1)) + ((DCH + 1) * b + 1))
                        ah, al = (v[:, k % 2, :].rearrange("p (t a s) -> p t a s", t=T, a=1)
                                  for v in (a_hi_sb, a_lo_sb))
                        nc.vector.tensor_tensor(al, spread[:, :, bass.ds(i * VRAW + b, 1), :], ah.bitcast(F32),
                                                ALU.subtract)
                        for c in range(DCH):
                            dve.wait_ge(v_hi, i * (VRAW * (DCH + 1)) + ((DCH + 1) * b + c + 2))
                            slot = (DCH * k + c) % VSPLIT
                            nc.vector.tensor_tensor(v_lo_sb[:, slot, :], v_raw[:, k, c * CH:(c + 1) * CH],
                                                    v_hi_sb[:, slot, :].bitcast(F32), ALU.subtract).then_inc(v_lo, 1)
                        for q in range(2 * k, 2 * k + 2):
                            n = t * PICKS + q
                            dve.wait_ge(tail_in[q % VRING], i * (2 * VRAW * 16 // VRING) + 16 * (n // VRING + 1))
                            dve.wait_ge(tails_used, i * (2 * VRAW) + (n + VPRESET))
                            nc.vector.scalar_tensor_tensor(
                                out=resid[:, t, DENSE:], in0=tail_rows[q % VRING][:],
                                scalar=weight[:, t, bass.ds(i * (2 * VRAW) + q, 1)], in1=resid[:, t, DENSE:],
                                op0=ALU.mult, op1=ALU.add).then_inc(tails_used, 1)
            dve.wait_ge(tails_used, VPRESET + T * PICKS)
            dve.wait_ge(gain2_in, 32)
            row_stats((DCH,))
            for c in range(DCH):
                dve.wait_ge(v_used, VSPLIT + DCH * (BLOCKS - 1) + c + 1)
                for t in range(T):
                    cols = resid[:, t, c * CH:(c + 1) * CH]
                    last = nc.vector.scalar_tensor_tensor(out=cols, in0=cols, scalar=ALPHA, in1=ps[:, DCH * t + c, :],
                                                          op0=ALU.mult, op1=ALU.add)
                link(last)
                row_stats((c,))
            norm(1, gain2[:, 0, :], gain2[:, 1, :])

        @block.tensor
        def _(pe):
            def turn(first, b, src):
                if first + b >= 4:
                    pe.wait_ge(turned_lo, first + b - 3)
                for c in range(2):
                    for t in range(T):
                        k = 2 * b + c
                        last = nc.tensor.transpose(ps[:, 4 + b % 4, (2 * c + t) * P:(2 * c + t + 1) * P],
                                                   src(t)[:, k * P:(k + 1) * P], ident[:])
                last.then_inc(turned, 1)

            def unit(g, j, hi, lo):
                u = unit_of(g, j)
                pe.wait_ge(w_lo, u + 1)
                for a in range(PAIR):
                    k = PAIR * j + a
                    first, final = k == 0, k == KC - 1
                    for half, kind in enumerate(GROUPS[g][1]):
                        wh = w_hi_sb[:, u % SPLIT, a, 512 * half:512 * half + 512]
                        wl = w_lo_sb[:, u % SPLIT, a, 512 * half:512 * half + 512]
                        if kind == "R":
                            for t in range(T):
                                if first and g == OUT1:
                                    pe.wait_ge(evac, n_evac[g] - 3 + 2 * half + t)
                                o = ps[:, 2 * half + t, :]
                                xh, xl = (v[:, k, t * P:(t + 1) * P] for v in (hi, lo))
                                nc.tensor.matmul(o, xh, wh, start=first, stop=False)
                                nc.tensor.matmul(o, xh, wl, start=False, stop=False)
                                last = nc.tensor.matmul(o, xl, wh, start=False, stop=final)
                        else:
                            for b in range(4):
                                o = ps[:, 2 * half + b // 2, (b % 2) * S:(b % 2 + 1) * S]
                                wbh, wbl = wh[:, b * P:(b + 1) * P], wl[:, b * P:(b + 1) * P]
                                nc.tensor.matmul(o, wbh, hi[:, k, :], start=first and b % 2 == 0, stop=False,
                                                 skip_group_check=True)
                                nc.tensor.matmul(o, wbh, lo[:, k, :], start=False, stop=False,
                                                 skip_group_check=True)
                                last = nc.tensor.matmul(o, wbl, hi[:, k, :], start=False, stop=final,
                                                        skip_group_check=True)
                last.then_inc(w_used, 1)

            def turn_qk(i):
                for c in range(2):
                    for t in range(T):
                        k = 2 * i + c
                        src = q_rows[:, t, k * P:(k + 1) * P] if i < 4 else kv[:, t, c * P:(c + 1) * P]
                        last = nc.tensor.transpose(ps[:, 4 + i % 4, (2 * c + t) * P:(2 * c + t + 1) * P], src, ident[:])
                last.then_inc(qk_turned, 1)

            def score(n):
                if n:
                    pe.wait_ge(sc_read, n)
                if n < SWA_BATCHES:
                    t, g, rp = tile_group(n)
                    nk = keys_of(n)
                    for m in range(2):
                        for r in range(512 // nk):
                            block_ = 4 * g + 2 * rp + r
                            last = nc.tensor.matmul(ps[:, 4 + m, r * nk:(r + 1) * nk],
                                                    qT[64 * m:64 * m + 64, block_, t * P:(t + 1) * P],
                                                    kT[64 * m:64 * m + 64, g, 0:nk], start=True, stop=True)
                else:
                    t = n - SWA_BATCHES
                    for h in range(MHEADS):
                        last = nc.tensor.matmul(ps[:, 4 + h // 2, (h % 2) * S:(h % 2 + 1) * S],
                                                qmT[:, h, t * P:(t + 1) * P], kmT[:, h, :], start=True, stop=True)
                last.then_inc(sc_done, 1)

            def turn_probs(n, half):
                pe.wait_ge(probs_ready, n + 1)
                f = 2 * n + half
                if f:
                    pe.wait_ge(pt_out, f)
                for i in range(4):
                    c0 = (4 * half + i) * P
                    last = nc.tensor.transpose(ps[:, 6, i * P:(i + 1) * P], prob_slot(n)[:, c0:c0 + P], ident[:])
                last.then_inc(pt_done, 1)

            def weigh(n, half):
                f = 2 * n + half
                pe.wait_ge(pt_out, f + 1)
                if n == BATCHES - 1:
                    pe.wait_ge(sc_read, BATCHES)
                elif half == 0 and n:
                    pe.wait_ge(heads_lo, n)
                for i in range(4):
                    q = 4 * half + i
                    pr = pT[:, f % 2, i * P:(i + 1) * P]
                    if n < 2:
                        o = ps[64 * (q % 2):64 * (q % 2) + 64, 7, (q // 2) * P:(q // 2 + 1) * P]
                        vc = KV_W + HD * (2 * n + q // 4)
                        last = nc.tensor.matmul(o, kv[:, 0, vc:vc + HD], pr, start=True, stop=True)
                    elif n < SWA_BATCHES:
                        g = tile_group(n)[1]
                        h, c = q // 2, q % 2
                        o = ps[64 * (h % 2):64 * (h % 2) + 64, 7, (h // 2) * P:(h // 2 + 1) * P]
                        vc = KV_W + HD * (2 * g + h // 2)
                        last = nc.tensor.matmul(o, kv[:, c, vc:vc + HD], pr, start=(c == 0), stop=(c == 1))
                    else:
                        h, c = q // 2, q % 2
                        last = nc.tensor.matmul(ps[:, sum_bank(n), h * P:(h + 1) * P],
                                                vm[:, c, h * MHD:(h + 1) * MHD], pr,
                                                start=(c == 0), stop=(c == 1))
                last.then_inc(pv_done, 1)

            def peer_scores(t, b):
                for i in range(4):
                    r = 4 * b + i
                    last = nc.tensor.matmul(ps[:, s12_bank(t, b), i * P:(i + 1) * P],
                                            scores_sb[:, r, t * P:(t + 1) * P], keysT[:, r % 2, :],
                                            start=True, stop=True)
                last.then_inc(s12_done, 1)

            mem_rows = lambda t: scores_flat[:, t * D:(t + 1) * D]

            def after(g, j):
                u = unit_of(g, j)
                if (g, j) == (Q, 0):
                    pe.wait_ge(small_in, 16 * 5)
                    pe.wait_ge(turned_lo, 8)
                    for a in range(2):
                        last = nc.tensor.transpose(ps[:, 7, a * P:(a + 1) * P], keys_rows[:, a, :], ident[:])
                    last.then_inc(keys_turned, 1)
                if (g, j) == (Q, 3):
                    pe.wait_ge(keys_out, 1)
                if g == Q:
                    pe.wait_ge(mem_in, 16)
                    turn(8, j, mem_rows)
                if (g, j) == (KV, 6):
                    pe.wait_ge(roped, T)
                    pe.wait_ge(turned_lo, 16)
                    for i in range(4):
                        turn_qk(i)
                if (g, j) == (POOLQM, 0):
                    pe.wait_ge(roped, 2 * T)
                    pe.wait_ge(qk_out, 1)
                    turn_qk(4)
                if (g, j) == (POOLQM, 2):
                    pe.wait_ge(qk_out, 5)
                if u == POOL_TURN:
                    pe.wait_ge(pooled, 4)
                    pe.wait_ge(w_pool_in, 16)
                    pe.wait_ge(sc_read, sum(s < u for s in SCORED))
                    for i in range(4):
                        last = nc.tensor.matmul(ps[:, 4 + i // 2, (i % 2) * S:(i % 2 + 1) * S], w_pool_sb[:, i, :],
                                                means[:, i, :], start=True, stop=True)
                    last.then_inc(pool_done, 1)
                for n in range(BATCHES):
                    if u == at(n, "sum1"):
                        weigh(n, 1)
                    if u == at(n, "turn1"):
                        weigh(n, 0)
                        turn_probs(n, 1)
                    if u == at(n, "turn0"):
                        turn_probs(n, 0)
                    if u == SCORED[n]:
                        if n == SWA_BATCHES:
                            pe.wait_ge(evac, n_evac[OUT0])
                        if u > POOL_TURN:
                            pe.wait_ge(pool_lo, 4)
                        score(n)
                if (g, j) == (PEER1, 1):
                    for t in range(T):
                        for b in range(2):
                            peer_scores(t, b)

            pe.wait_ge(consts, 4)
            for b in range(KC // 2):
                if b % 4 == 0:
                    pe.wait_ge(x_in[b // 4], 16)
                turn(0, b, lambda t: resid[:, t, :])
            for g in range(len(GROUPS)):
                if g and g != OUT1:
                    pe.wait_ge(evac, n_evac[g])
                if g == PEER0:
                    for b in range(KC // 2):
                        if b % 2 == 0:
                            pe.wait_ge(normed, T * (b // 2 + 1))
                        turn(16, b, lambda t: resid[:, t, :])
                hi, lo = (yT_hi, yT_lo) if g in (MEM, PEER0, PEER1) else (xT_hi, xT_lo)
                for j in range(UNITS):
                    if g == Q:
                        pe.wait_ge(turned_lo, j + 1)
                    if g == PEER0:
                        pe.wait_ge(turned_lo, 16 + j + 1)
                    if g == OUT0 and j % 2 == 0:
                        pe.wait_ge(*((pool_lo, 4), (heads_lo, 4), (heads_lo, 6), (heads_lo, 8))[j // 2])
                    unit(g, j, hi, lo)
                    after(g, j)
            pe.wait_ge(evac, n_evac[PEER1 + 1])
            for t in range(T):
                for b in range(2, 4):
                    peer_scores(t, b)

            pe.sem_inc(built, ONES)
            pe.sem_inc(v_used, VSPLIT)
            pe.wait_ge(s12_out, 8)
            for t in range(T):
                pe.wait_ge(weighted, t + 1)
                for a in range(3):
                    src = chosen[:, t, a].rearrange("p h k -> p (h k)") if a < 2 else weight[:, t, :]
                    last = nc.tensor.transpose(ps[:, t, a * P:(a + 1) * P], src, ident[:])
                last.then_inc(pair_turned, 1)
                with pe.Fori(0, P // 16) as i:
                    for k in range(16):
                        n = t * P + k
                        if k % 4 == 0:
                            pe.wait_ge(spread_out, i * 4 + (n // 4 + 1))
                        if k % HOT == 0:
                            pe.wait_ge(hot_weights, i * (16 // HOT) + (n // HOT + 1))
                        nc.tensor.matmul(ps[:, 4 + k // 4, (k % 4) * P:(k % 4 + 1) * P], hot[:, 1, k, :],
                                         hot[:, 0, k, :], start=True, stop=True).then_inc(built, 1)
            pe.wait_ge(spread_out, 4 + S // 4)

            def blocks(i, first, final):
                for k in range(VRAW):
                    for c in range(DCH):
                        n = DCH * k + c
                        pe.wait_ge(v_lo, i * (VRAW * DCH) + (VRAW * DCH + n + 1))
                        for t in range(T):
                            ah, al = (v[:, k % 2, t * P:(t + 1) * P] for v in (a_hi_sb, a_lo_sb))
                            vh, vl = v_hi_sb[:, n % VSPLIT, :], v_lo_sb[:, n % VSPLIT, :]
                            o = ps[:, DCH * t + c, :]
                            nc.tensor.matmul(o, ah, vh, start=first and k == 0, stop=False)
                            nc.tensor.matmul(o, ah, vl, start=False, stop=False)
                            last = nc.tensor.matmul(o, al, vh, start=False, stop=final and k == VRAW - 1)
                        last.then_inc(v_used, 1)

            turns = BLOCKS // VRAW
            blocks(0, True, False)
            with pe.Fori(1, turns - 1) as i:
                blocks(i, False, False)
            blocks(turns - 1, False, True)


_INS = ["x", "mem", "positions", "w_in", "w_mem_kv", "w_pool", "pool_scale", "attn_sinks", "w_out", "ln1_g", "ln1_b",
        "w_peer_q", "sub_keys_1", "sub_keys_2", "expert_u", "expert_v", "ln2_g", "ln2_b"]


def kernel(**inputs):
    import numpy as np
    import concourse.bacc as bacc
    from concourse.bass_utils import run_bass_kernel_spmd

    nc = bacc.Bacc("TRN2", target_bir_lowering=False, num_devices=1)
    arrays, args = {}, []
    for name in _INS:
        a = np.ascontiguousarray(inputs[name])
        arrays[name] = a
        args.append(nc.dram_tensor(name, a.shape, mybir.dt.from_np(a.dtype), kind="ExternalInput").ap())
    args.append(nc.dram_tensor("out", (1, S, D), F32, kind="ExternalOutput").ap())
    hybrid_layer(nc, *args)
    got = run_bass_kernel_spmd(nc, [arrays], core_ids=[0])
    return got.results[0]["out"]
```
